# Optimizing a Trainium2 kernel written in Bass

```python
import math
import jax, jax.numpy as jnp
from jax import lax
import numpy as np

D_MODEL = 1024
BATCH = 1
SEQ = 512
DEPTH = 2

RET_HEADS = 4
RET_QK_DIM = 128
RET_V_DIM = 256
RET_QK_W = RET_HEADS * RET_QK_DIM
RET_V_W = RET_HEADS * RET_V_DIM
RET_CHUNK = 128
ROPE_BASE = 10000.0
POOL_WINDOWS = (2, 4, 8, 16)
POOL_GROUPS = 4
POOL_GROUP_DIM = D_MODEL // 8
POOL_W = POOL_GROUPS * POOL_GROUP_DIM
N_BRANCH = 2
IN_W = 2 * RET_QK_W + 2 * RET_V_W + POOL_W + N_BRANCH * D_MODEL
IN_SPLITS = (RET_QK_W, 2 * RET_QK_W, 2 * RET_QK_W + RET_V_W, 2 * RET_QK_W + 2 * RET_V_W,
             2 * RET_QK_W + 2 * RET_V_W + POOL_W, 2 * RET_QK_W + 2 * RET_V_W + POOL_W + D_MODEL)
N_EXPERTS = 16
N_GROUPS = 4
EXPERTS_PER_GROUP = N_EXPERTS // N_GROUPS
TOP_K = 2
D_EXPERT = D_MODEL // 2
MOE_BLOCK = 256
EPS = 1e-6

kernel_name = "hybrid_retention_pool_grouped_moe_adaln"

def rmsnorm(x, g):
    xf = x.astype(jnp.float32)
    y = xf * lax.rsqrt(jnp.mean(xf * xf, axis=-1, keepdims=True) + EPS)
    return y.astype(x.dtype) * g

def modulate(h, shift, scale):
    return h * (1.0 + scale[:, None, :]) + shift[:, None, :]

def rotary(t, pos):
    d = t.shape[-1]
    freqs = ROPE_BASE ** (-jnp.arange(0, d, 2, dtype=jnp.float32) / d)
    ang = pos[:, None] * freqs[None, :]
    cos = jnp.cos(ang).astype(t.dtype)
    sin = jnp.sin(ang).astype(t.dtype)
    t1, t2 = t[..., : d // 2], t[..., d // 2:]
    return jnp.concatenate([t1 * cos - t2 * sin, t1 * sin + t2 * cos], axis=-1)

def retention_chunkwise(q, k, v):
    b, h, s, dk = q.shape
    dv = v.shape[-1]
    c = RET_CHUNK
    n = s // c
    dt = q.dtype
    log_gamma = jnp.log(1.0 - 2.0 ** (-5.0 - jnp.arange(h, dtype=jnp.float32)))
    idx = jnp.arange(c, dtype=jnp.float32)
    rel = idx[:, None] - idx[None, :]
    causal = rel >= 0
    decay_in = jnp.where(causal[None], jnp.exp(log_gamma[:, None, None] * jnp.where(causal, rel, 0.0)[None]), 0.0)
    xi = jnp.exp(log_gamma[:, None] * (idx[None, :] + 1.0))
    zeta = jnp.exp(log_gamma[:, None] * (c - 1.0 - idx[None, :]))
    gamma_c = jnp.exp(log_gamma * c).astype(dt)
    qc = q.reshape(b, h, n, c, dk)
    kc = k.reshape(b, h, n, c, dk)
    vc = v.reshape(b, h, n, c, dv)
    scores = jnp.einsum('bhncd,bhnmd->bhncm', qc, kc) * decay_in[None, :, None].astype(dt)
    y_inner = jnp.einsum('bhncm,bhnme->bhnce', scores, vc)
    kv = jnp.einsum('bhnmd,bhnme->nbhde', kc * zeta[None, :, None, :, None].astype(dt), vc)

    def step(state, kv_n):
        return state * gamma_c[None, :, None, None] + kv_n, state

    _, prev = lax.scan(step, jnp.zeros((b, h, dk, dv), dt), kv)
    y_cross = jnp.einsum('bhncd,nbhde->bhnce', qc * xi[None, :, None, :, None].astype(dt), prev)
    return (y_inner + y_cross).reshape(b, h, s, dv)

def head_norm(y):
    yf = y.astype(jnp.float32)
    return (yf * lax.rsqrt(jnp.mean(yf * yf, axis=-1, keepdims=True) + EPS)).astype(y.dtype)

def multiscale_pool(u, pool_w, pool_scale):
    b, s, _ = u.shape
    ug = u.reshape(b, s, POOL_GROUPS, POOL_GROUP_DIM)
    cs = jnp.cumsum(ug.astype(jnp.float32), axis=1)
    cs = jnp.pad(cs, ((0, 0), (1, 0), (0, 0), (0, 0)))
    t = jnp.arange(s)
    win = jnp.array(POOL_WINDOWS, dtype=jnp.int32)
    lo = jnp.maximum(t[:, None] + 1 - win[None, :], 0)
    gidx = jnp.arange(POOL_GROUPS)[None, :]
    window_sum = cs[:, 1:] - cs[:, lo, gidx]
    count = jnp.minimum(t[:, None] + 1, win[None, :]).astype(jnp.float32)
    mix = (window_sum / count[None, :, :, None] - ug.astype(jnp.float32)).astype(u.dtype)
    y = jnp.einsum('bsgc,gcd->bsgd', mix, pool_w).reshape(b, s, POOL_W)
    return y * pool_scale

def mixer(h, w_in, w_ret_o, pool_w, pool_scale, w_pool_o, w_out):
    b, s, _ = h.shape
    proj = h @ w_in
    q, k, v, g, u, a_ret, a_pool = jnp.split(proj, IN_SPLITS, axis=-1)

    def heads(t, d):
        return t.reshape(b, s, RET_HEADS, d).transpose(0, 2, 1, 3)

    pos = jnp.arange(s, dtype=jnp.float32)
    qh = rotary(heads(q, RET_QK_DIM), pos)
    kh = rotary(heads(k, RET_QK_DIM), pos) * (RET_QK_DIM ** -0.5)
    y = retention_chunkwise(qh, kh, heads(v, RET_V_DIM))
    y = head_norm(y).transpose(0, 2, 1, 3).reshape(b, s, RET_V_W)
    y_ret = (jax.nn.silu(g) * y) @ w_ret_o
    y_pool = multiscale_pool(u, pool_w, pool_scale) @ w_pool_o
    merged = jax.nn.sigmoid(a_ret) * y_ret + jax.nn.sigmoid(a_pool) * y_pool
    return merged @ w_out

def route(hf, w_router, b_router):
    t = hf.shape[0]
    logits = (hf @ w_router).astype(jnp.float32) + b_router.astype(jnp.float32)
    probs = jax.nn.softmax(logits, axis=-1)
    grouped = probs.reshape(t, N_GROUPS, EXPERTS_PER_GROUP)
    group_score = lax.top_k(grouped, TOP_K)[0].sum(-1)
    sel_group = jnp.argmax(group_score, axis=-1)
    in_group = jnp.take_along_axis(grouped, sel_group[:, None, None], axis=1)[:, 0]
    top_p, top_local = lax.top_k(in_group, TOP_K)
    expert_idx = sel_group[:, None] * EXPERTS_PER_GROUP + top_local
    weights = top_p / jnp.sum(top_p, axis=-1, keepdims=True)
    return expert_idx, weights

def moe(h, w_router, b_router, w_gate, w_up, w_down):
    b, s, d = h.shape
    t = b * s
    hf = h.reshape(t, d)
    expert_idx, weights = route(hf, w_router, b_router)
    a = t * TOP_K
    e_flat = expert_idx.reshape(a)
    tok_flat = jnp.arange(a, dtype=jnp.int32) // TOP_K
    w_flat = weights.reshape(a)
    order = jnp.argsort(e_flat)
    e_sorted = e_flat[order]
    counts = jnp.bincount(e_flat, length=N_EXPERTS)
    padded = ((counts + MOE_BLOCK - 1) // MOE_BLOCK) * MOE_BLOCK
    start = jnp.cumsum(counts) - counts
    pad_end = jnp.cumsum(padded)
    pad_start = pad_end - padded
    dest = pad_start[e_sorted] + (jnp.arange(a) - start[e_sorted])
    n_slots = a + N_EXPERTS * MOE_BLOCK
    n_blocks = n_slots // MOE_BLOCK
    slot_tok = jnp.zeros((n_slots,), jnp.int32).at[dest].set(tok_flat[order])
    slot_w = jnp.zeros((n_slots,), jnp.float32).at[dest].set(w_flat[order])
    block_e = jnp.minimum(jnp.searchsorted(pad_end, jnp.arange(n_blocks) * MOE_BLOCK, side='right'), N_EXPERTS - 1)
    xb = hf[slot_tok].reshape(n_blocks, MOE_BLOCK, d)

    def expert_block(args):
        xblk, e = args
        return (jax.nn.silu(xblk @ w_gate[e]) * (xblk @ w_up[e])) @ w_down[e]

    yb = lax.map(expert_block, (xb, block_e))
    y_slots = yb.reshape(n_slots, d) * slot_w[:, None].astype(yb.dtype)
    return jax.ops.segment_sum(y_slots, slot_tok, num_segments=t).reshape(b, s, d)

def setup_inputs(seed: int = 0) -> dict:
    key = jax.random.key(seed)
    ks = jax.random.split(key, 20)
    f32 = jnp.float32
    nrm = lambda k, shape, sc: jax.random.normal(k, shape, f32) * sc
    return {
        "x": nrm(ks[0], (BATCH, SEQ, D_MODEL), 1.0),
        "c": nrm(ks[1], (BATCH, D_MODEL), 1.0),
        "w_ada": nrm(ks[2], (DEPTH, D_MODEL, 6 * D_MODEL), 0.5 * D_MODEL ** -0.5),
        "b_ada": nrm(ks[3], (DEPTH, 6 * D_MODEL), 0.02),
        "norm1_g": 1.0 + nrm(ks[4], (DEPTH, D_MODEL), 0.02),
        "norm2_g": 1.0 + nrm(ks[5], (DEPTH, D_MODEL), 0.02),
        "w_in": nrm(ks[6], (DEPTH, D_MODEL, IN_W), D_MODEL ** -0.5),
        "w_ret_o": nrm(ks[7], (DEPTH, RET_V_W, D_MODEL), RET_V_W ** -0.5),
        "pool_w": nrm(ks[8], (DEPTH, POOL_GROUPS, POOL_GROUP_DIM, POOL_GROUP_DIM), POOL_GROUP_DIM ** -0.5),
        "pool_scale": 1.0 + nrm(ks[9], (DEPTH, POOL_W), 0.1),
        "w_pool_o": nrm(ks[10], (DEPTH, POOL_W, D_MODEL), POOL_W ** -0.5),
        "w_out": nrm(ks[11], (DEPTH, D_MODEL, D_MODEL), D_MODEL ** -0.5),
        "w_router": nrm(ks[12], (D_MODEL, N_EXPERTS), D_MODEL ** -0.5),
        "b_router": nrm(ks[13], (N_EXPERTS,), 0.01),
        "w_e_gate": nrm(ks[14], (DEPTH, N_EXPERTS, D_MODEL, D_EXPERT), D_MODEL ** -0.5),
        "w_e_up": nrm(ks[15], (DEPTH, N_EXPERTS, D_MODEL, D_EXPERT), D_MODEL ** -0.5),
        "w_e_down": nrm(ks[16], (DEPTH, N_EXPERTS, D_EXPERT, D_MODEL), D_EXPERT ** -0.5),
        "final_g": 1.0 + nrm(ks[17], (D_MODEL,), 0.02),
    }

def reference(x, c, w_ada, b_ada, norm1_g, norm2_g, w_in, w_ret_o, pool_w, pool_scale, w_pool_o, w_out,
              w_router, b_router, w_e_gate, w_e_up, w_e_down, final_g):
    cond = jax.nn.silu(c)
    for l in range(DEPTH):
        mod = cond @ w_ada[l] + b_ada[l]
        sh1, sc1, g1, sh2, sc2, g2 = jnp.split(mod, 6, axis=-1)
        h = modulate(rmsnorm(x, norm1_g[l]), sh1, sc1)
        x = x + g1[:, None, :] * mixer(h, w_in[l], w_ret_o[l], pool_w[l], pool_scale[l], w_pool_o[l], w_out[l])
        h = modulate(rmsnorm(x, norm2_g[l]), sh2, sc2)
        x = x + g2[:, None, :] * moe(h, w_router, b_router, w_e_gate[l], w_e_up[l], w_e_down[l])
    return rmsnorm(x, final_g)


_drawn_inputs = setup_inputs


def setup_inputs(seed=0):
    import zlib

    import numpy as np

    out = dict(_drawn_inputs(seed))
    spreads = {}
    factors = {}
    for name, (base, spread) in spreads.items():
        noise = np.random.default_rng([zlib.crc32(name.encode()), seed]).standard_normal(out[name].shape)
        drawn = base * np.exp(spread * noise) if base else spread * noise
        out[name] = __import__('jax').numpy.asarray(drawn.astype(out[name].dtype))
    for name, factor in factors.items():
        out[name] = (out[name] * factor).astype(out[name].dtype)
    return out
```

```python
from contextlib import ExitStack

import numpy as np

import concourse.bass as bass
from concourse import mybir

F32 = mybir.dt.float32
F32R = mybir.dt.float32r
I32 = mybir.dt.int32
ALU = mybir.AluOpType
ACT = mybir.ActivationFunctionType
AX = mybir.AxisListType.X

P = 128
D = 1024
T = 512
DEPTH = 2
NT = T // P
HEADS = 4
DK = 128
DV = 256
WINDOWS = (2, 4, 8, 16)
NE = 16
NG = 4
EPS = 1e-6
CAP = 128
LEVELS = T // CAP
NOV = 2 * T // CAP - 1
NSLOT = (NE + NOV) * CAP

GROUPS = [("q", 4), ("k", 4), ("v0", 4), ("v1", 4), ("u", 4), ("g0", 4), ("g1", 4), ("ap0", 4), ("P0", 2),
          ("ap1", 4), ("P1", 2), ("ar0", 4), ("R0", 4), ("ar1", 4), ("R1", 4), ("O0", 4), ("O1", 4)]
NAMES = [g for g, _ in GROUPS]
W_IN_COLUMN = {"q": 0, "k": 1, "v0": 2, "v1": 3, "g0": 4, "g1": 5, "u": 6, "ar0": 7, "ar1": 8, "ap0": 9, "ap1": 10}
FIRST = {g: sum(n for _, n in GROUPS[:i]) for i, (g, _) in enumerate(GROUPS)}
LAST = {g: FIRST[g] + n - 1 for g, n in GROUPS}
NGROUP = len(GROUPS)
MIX = sum(n for _, n in GROUPS)
EXP = 12
PROD = MIX + EXP * NE
NADA = 12
ADA_PIECES = 4
RAW_SLOTS = 8
W_SLOTS = 4
PRE = 4 * ADA_PIECES
RAW_MIX = MIX + NADA * ADA_PIECES
RAW = RAW_MIX + EXP * NE
PIECES = PRE + DEPTH * RAW


def layer_stream():
    out = [("w", q) for q in range(W_SLOTS)]
    for q in range(MIX):
        ends = [i for i, g in enumerate(NAMES) if LAST[g] == q]
        if ends and ends[0] < NADA:
            out += [("ada", ends[0], j) for j in range(ADA_PIECES)]
        if q + W_SLOTS < MIX:
            out.append(("w", q + W_SLOTS))
    return out


STREAM = layer_stream()
RAW_OF_W = {s[1]: r for r, s in enumerate(STREAM) if s[0] == "w"}
RAW_OF_ADA = {s[1:]: r for r, s in enumerate(STREAM) if s[0] == "ada"}

UNIT_LIST = [("h1", 8), ("q", 4), ("k", 4), ("mix", 4), ("y", 8), ("pw", 4), ("m0", 4), ("m1", 4), ("h2", 8)]
UNITS = dict(UNIT_LIST)
UNIT0 = {name: sum(n for _, n in UNIT_LIST[:i]) for i, (name, _) in enumerate(UNIT_LIST)}
NUNIT = sum(UNITS.values())
SPLIT_LIST = [u for u in UNIT_LIST if u[0] not in ("q", "k", "mix")]
SPLIT0 = {name: sum(n for _, n in SPLIT_LIST[:i]) for i, (name, _) in enumerate(SPLIT_LIST)}
NSPLIT = sum(n for _, n in SPLIT_LIST)

CONST_WIDTH = [("ident", P), ("causal", P), ("before", P), ("ones", P), ("iota", P), ("diag", 4 * P),
               ("diag0", 64), ("off", 64), ("xi", 4), ("vscale", 4), ("tokid", 4), ("rev16", 16), ("rev4", 4),
               ("ecap", 16), ("blockid", NOV), ("eid", 16), ("eps", 1), ("wr", 8 * NE), ("br", NE)]
CONST_AT = {}
NCONST = 0
for _name, _n in CONST_WIDTH:
    CONST_AT[_name] = (NCONST, _n)
    NCONST += _n
GAMMA = [1.0 - 2.0 ** (-5.0 - h) for h in range(HEADS)]
GAMMA_C = [g ** P for g in GAMMA]


def constants():
    c = np.zeros((P, NCONST), np.float32)

    def put(name, a):
        o, n = CONST_AT[name]
        c[:, o:o + n] = np.asarray(a, np.float64).reshape(P, n)

    i = np.arange(P)
    put("ident", np.eye(P))
    put("causal", (i[None, :] >= i[:, None]))
    put("before", (i[:, None] < i[None, :]))
    put("ones", np.ones((P, P)))
    put("iota", np.tile(i, (P, 1)))
    diag, diag0, off = np.zeros((P, 4, P)), np.zeros((P, 4, 16)), np.zeros((P, 4, 16))
    for g, w in enumerate(WINDOWS):
        a = np.zeros((2 * P, 2 * P))
        for s in range(2 * P):
            lo = max(s + 1 - w, 0)
            a[s, lo:s + 1] = np.float32(1.0) / np.float32(s + 1 - lo)
            a[s, s] -= 1.0
        diag[:, g], diag0[:, g], off[:, g] = a[P:, P:].T, a[:16, :P].T, a[P:P + 16, :P].T
    put("diag", diag)
    put("diag0", diag0)
    put("off", off)
    g = np.array(GAMMA)
    put("xi", g[None, :] ** (i[:, None] + 1.0))
    put("vscale", g[None, :] ** -(i[:, None] + 1.0) * DK ** -0.5)
    put("tokid", i[:, None] + P * np.arange(NT)[None, :])
    put("rev16", np.tile(16 - np.arange(16), (P, 1)))
    put("rev4", np.tile(4 - np.arange(4), (P, 1)))
    put("ecap", np.tile(CAP * np.arange(16), (P, 1)))
    put("blockid", np.tile(np.arange(NOV), (P, 1)))
    put("eid", np.tile(np.arange(16), (P, 1)))
    put("eps", np.full((P, 1), EPS))
    return c


def rotary_tables():
    freqs = np.float32(10000.0) ** (-np.arange(0, DK, 2, dtype=np.float32) / np.float32(DK))
    ang = (np.arange(T, dtype=np.float32)[:, None] * freqs[None, :]).astype(np.float32).astype(np.float64)
    cos, sin = np.cos(ang), np.sin(ang)
    both = np.stack([np.concatenate([cos, cos], 1), np.concatenate([-sin, sin], 1)])
    return np.ascontiguousarray(both.reshape(2, NT, P, DK).transpose(2, 0, 1, 3).astype(np.float32))


def build(nc, w, x_in, c_in, consts, rotary, ada_rows, pool_w, pool_scale, final_g, out):
    mod = nc.dram_tensor("mod_rows", (4 + DEPTH * NADA, 512), F32, kind="Internal").ap()
    x_state = nc.dram_tensor("x_state", (P, NT * D), F32, kind="Internal").ap()
    h_rows = nc.dram_tensor("h_rows", (T, D), F32, kind="Internal").ap()
    y_rows = nc.dram_tensor("y_rows", (NSLOT, D), F32, kind="Internal").ap()

    with ExitStack() as ctx:
        def sem(name):
            return ctx.enter_context(nc.semaphore(name))

        at = (nc.sbuf_base + 63) // 64 * 64

        def region(kib):
            nonlocal at
            at += int(kib * 1024)
            return at - int(kib * 1024)

        def sb(name, shape, dtype, offset):
            return nc.alloc_sbuf_tensor_at(name, shape, dtype, offset=offset)

        raw = sb("raw", [P, RAW_SLOTS, 1024], F32, region(32))
        w_hi = sb("w_hi", [P, W_SLOTS, 1024], F32R, region(16))
        w_lo = sb("w_lo", [P, W_SLOTS, 1024], F32R, region(16))
        hT_hi = sb("hT_hi", [P, 8, T], F32R, region(16))
        hT_lo = sb("hT_lo", [P, 8, T], F32R, region(16))

        A = region(32)
        q_rot = sb("q_rot", [P, NT, 512], F32, A)
        k_rot = sb("k_rot", [P, NT, 512], F32, A + 8192)
        qT = sb("qT", [P, HEADS, T], F32, A + 16384)
        kT = sb("kT", [P, HEADS, T], F32, A + 24576)
        yT_hi = sb("yT_hi", [P, 8, T], F32R, A)
        yT_lo = sb("yT_lo", [P, 8, T], F32R, A + 16384)
        xg = sb("xg", [P, 2, D], F32, A)
        xgT_hi = sb("xgT_hi", [P, 2, D], F32R, A + 8192)
        xgT_lo = sb("xgT_lo", [P, 2, D], F32R, A + 16384)
        hid = sb("hid", [P, 512], F32, A + 24576)
        hidT_hi = sb("hidT_hi", [P, 512], F32R, A + 26624)
        hidT_lo = sb("hidT_lo", [P, 512], F32R, A + 28672)
        y_pair = sb("y_pair", [P, 2, 2, D], F32, A)
        o_hot = sb("o_hot", [P, 8, P], F32, A)
        o_x = sb("o_x", [P, D], F32, A + 4096)
        o_xT = sb("o_xT", [P, 8, P], F32, A + 8192)
        o_w = sb("o_w", [P, 1024], F32, A + 12288)
        o_sig = sb("o_sig", [P, 2, 256], F32, A + 16384)
        o_hid = sb("o_hid", [P, 512], F32, A + 18432)
        o_hidT = sb("o_hidT", [P, 4, P], F32, A + 20480)
        hot = sb("hot", [P, 2, NT, P], F32, A + 24576)

        B = region(16)
        y = sb("y", [P, NT, D], F32, B)
        ypT_hi = sb("ypT_hi", [P, 4, T], F32R, B)
        ypT_lo = sb("ypT_lo", [P, 4, T], F32R, B + 8192)
        y_out = sb("y_out", [P, 2, D], F32, B)
        o_y = sb("o_y", [P, D], F32, B + 8192)

        C = region(16)
        x = sb("x", [P, NT, D], F32, C)
        rope = sb("rope", [P, 2, NT, DK], F32, C)
        u = sb("u", [P, NT, 512], F32, C)
        mixT = sb("mixT", [P, 4, T], F32, C + 8192)
        merged = sb("merged", [P, 2, NT, 512], F32, C)

        Dr = region(11)
        scores = sb("scores", [P, 2, T], F32, Dr)
        kv_sum = sb("kv_sum", [P, 3, DV], F32, Dr + 4096)
        state = sb("state", [P, 3, DV], F32, Dr + 7168)
        y_sq = sb("y_sq", [P, DV], F32, Dr + 10240)
        h_nat = sb("h_nat", [P, 2, D], F32, Dr)
        sig_ret = sb("sig_ret", [P, NT, 512], F32, Dr)

        shift_row = sb("shift_row", [P, D], F32, region(4))
        scale_row = sb("scale_row", [P, D], F32, region(4))
        gate_row = sb("gate_row", [P, D], F32, region(4))
        ada_acc = sb("ada_acc", [P, 512], F32, region(2))
        ada_add = sb("ada_add", [1, 2, 512], F32, region(4))
        ada_row = sb("ada_row", [1, 512], F32, region(2))
        tmp = sb("tmp", [P, 2, 512], F32, region(4))
        const = sb("const", [P, NCONST], F32, region((NCONST * 4 + 1023) // 1024))
        pw = sb("pw", [P, 4, P], F32, region(2))

        def small(name, n, dtype=F32):
            return sb(name, [P, n], dtype, region(((n * 4 + 63) // 64) * 64 / 1024))

        router_at = A + 8192

        def router_small(name, n):
            nonlocal router_at
            router_at += (n * 4 + 63) // 64 * 64
            return sb(name, [P, n], F32, router_at - (n * 4 + 63) // 64 * 64)

        pscale = small("pscale", 4)
        cond = small("cond", 8)
        cond_raw = small("cond_raw", 8)
        wr_hi = small("wr_hi", 8 * NE, F32R)
        wr_lo = small("wr_lo", 8 * NE, F32R)
        y_ss = small("y_ss", 16)
        y_std = small("y_std", 16)
        y_rs = small("y_rs", 16)
        x_ss = small("x_ss", 4)
        x_std = small("x_std", 4)
        x_rs = small("x_rs", 4)
        lg = router_small("lg", 64)
        probs = router_small("probs", 64)
        s4 = router_small("s4", 16)
        s4b = router_small("s4b", 16)
        rt = router_small("rt", 64)
        pairs = router_small("pairs", 96)
        r1 = router_small("r1", 4)
        top = router_small("top", 8)
        wts = small("wts", 8)
        hot1 = router_small("hot1", 64)
        hot2 = router_small("hot2", 64)
        chosen = router_small("chosen", 64)
        pos = router_small("pos", 64)
        ovn = router_small("ovn", 16)
        ovc = router_small("ovc", 32)
        ovd = router_small("ovd", 32)
        slotf = small("slotf", 8)
        posk = router_small("posk", 8)
        hotid = router_small("hotid", 128)
        ovt = router_small("ovt", 16 * NOV)
        ovt2 = router_small("ovt2", 16 * NOV)
        ov_range_f = small("ov_range_f", 2)
        ov_base = small("ov_base", 1)
        slot_i = small("slot_i", 8, I32)
        idx = small("idx", 16, I32)
        ov_range = small("ov_range", 2, I32)
        ov_expert = small("ov_expert", NOV, I32)
        o_idx = small("o_idx", 1, I32)
        idx_next = small("idx_next", 2, I32)
        assert at <= 229344, at

        def k(name):
            o, n = CONST_AT[name]
            return const[:, o:o + n]

        ps = ctx.enter_context(nc.psum_tensor("ps", [P, 8, 512], F32))
        ident = k("ident")

        landed = [sem(f"raw_landed{s}") for s in range(RAW_SLOTS)]
        raw_used = sem("raw_used")
        w_hi_ready = sem("w_hi_ready")
        w_used = sem("w_used")
        acc_ready = sem("acc_ready")
        acc_free = sem("acc_free")
        unit_ready = sem("unit_ready")
        unit_hi = sem("unit_hi")
        unit_free = sem("unit_free")
        x_landed = sem("x_landed")
        c_landed = sem("c_landed")
        consts_landed = sem("consts_landed")
        cond_sig = sem("cond_sig")
        wr_hi_ready = sem("wr_hi_ready")
        x_std_ready = sem("x_std_ready")
        h_ready = sem("h_ready")
        rot_done = sem("rot_done")
        score_ready = sem("score_ready")
        score_masked = sem("score_masked")
        kv_ready = sem("kv_ready")
        kv_used = sem("kv_used")
        state_ready = sem("state_ready")
        y_ready = sem("y_ready")
        y_read = sem("y_read")
        y_std_ready = sem("y_std_ready")
        gate_sig = sem("gate_sig")
        gated = sem("gated")
        merged_add = sem("merged_add")
        x_added = sem("x_added")
        x_final = sem("x_final")
        ada_mac = sem("ada_mac")
        ada_sum = sem("ada_sum")
        ada_row_ready = sem("ada_row_ready")
        ada_add_landed = sem("ada_add_landed")
        mod_stored = [sem(f"mod_stored{i}") for i in range(2)]
        x_saved = sem("x_saved")
        x_back = sem("x_back")
        rope_landed = sem("rope_landed")
        pw_landed = sem("pw_landed")
        norm_rows = sem("norm_rows")
        gate_landed = sem("gate_landed")
        row_stored = [sem(f"row_stored{i}") for i in range(2)]
        logits_ready = sem("logits_ready")
        max_off = sem("max_off")
        exp_done = sem("exp_done")
        chosen_ready = sem("chosen_ready")
        pos_ready = sem("pos_ready")
        hot_ready = sem("hot_ready")
        idx_sum = sem("idx_sum")
        idx_ready = sem("idx_ready")
        gathered = [sem(f"gathered{i}") for i in range(2)]
        xgT_ready = sem("xgT_ready")
        xgT_hi_ready = sem("xgT_hi_ready")
        xgT_lo_ready = sem("xgT_lo_ready")
        act_sig = sem("act_sig")
        hid_ready = sem("hid_ready")
        hidT_ready = sem("hidT_ready")
        hidT_hi_ready = sem("hidT_hi_ready")
        hidT_lo_ready = sem("hidT_lo_ready")
        y_copied = sem("y_copied")
        pair_in = [[sem(f"pair_in{i}{j}") for j in range(2)] for i in range(2)]
        pair_scaled = sem("pair_scaled")
        ov_step = sem("ov_step")
        ov_w = sem("ov_w")
        ov_x = sem("ov_x")
        ov_y = sem("ov_y")
        norm_done = sem("norm_done")
        y_filled = sem("y_filled")
        out_stored = sem("out_stored")
        steps = sem("steps")

        block = ctx.enter_context(nc.Block())

        def land_value(l, r):
            return l * (16 * RAW // RAW_SLOTS) + 16 * ((PRE + r) // RAW_SLOTS + 1)

        def raw_value(l, r):
            return l * RAW + (PRE + r + 1 + RAW_SLOTS)

        def w_done(l, q):
            return l * PROD + (q + 1 + W_SLOTS)

        def acc_value(l, g, t):
            return l * (4 * NGROUP) + (4 * g + t + 1 + 4)

        def unit_value(l, name, n):
            return l * NUNIT + (UNIT0[name] + n + 1)

        OV_STEPS = 22
        FILLS = 16 * -(-NOV * CAP // T)

        def apart(eng):
            eng.sem_inc(steps, 1)

        @block.sync
        def _(sp):
            with sp.Fori(0, PIECES // RAW_SLOTS) as i:
                for s in range(RAW_SLOTS):
                    sp.wait_ge(raw_used, i * RAW_SLOTS + (s + 1))
                    sp.dma_start(raw[:, s], w[bass.ds(i * RAW_SLOTS + s, 1)].rearrange("o p n -> (o p) n")
                                 ).then_inc(landed[s], 16)

        def overflow_blocks(eng, l):
            apart(eng)
            start = eng.value_load(ov_range[0:1, 0:1], min_val=0, max_val=DEPTH * NOV)
            count = eng.value_load(ov_range[0:1, 1:2], min_val=0, max_val=NOV)
            return start, count

        @block.scalar
        def _(act):
            act.sem_inc(state_ready, 3)
            act.sem_inc(y_copied, 1)
            act.wait_ge(consts_landed, 16)
            act.activation(wr_hi[:], k("wr"), ACT.Copy).then_inc(wr_hi_ready, 1)
            act.wait_ge(c_landed, 16)
            act.activation(cond[:], cond_raw[:], ACT.Sigmoid).then_inc(cond_sig, 1)

            def hi(l, q, r):
                act.wait_ge(landed[r % RAW_SLOTS], land_value(l, r))
                act.wait_ge(w_used, l * PROD + (q + 1))
                act.activation(w_hi[:, q % W_SLOTS], raw[:, r % RAW_SLOTS], ACT.Copy).then_inc(w_hi_ready, 1)

            def row_deviations(l, which):
                for t in range(NT):
                    act.activation(h_nat[:, t % 2], x[:, t], ACT.Square, accum_out=x_ss[:, t:t + 1])
                    act.drain()
                act.activation(x_std[:], x_ss[:], ACT.Sqrt, bias=k("eps"), scale=1.0 / D).then_inc(x_std_ready, 1)

            def unit_hi_half(l, name, n, dst, scale=1.0):
                act.wait_ge(unit_ready, unit_value(l, name, n))
                bank = 4 + (UNIT0[name] + n) % 2
                act.activation(dst, ps[:, bank].rearrange("p (a b) -> p a b", a=4) if len(dst.shape) == 3 else ps[:, bank],
                               ACT.Copy, scale=scale).then_inc(unit_hi, 1)

            def transposed_hi(l, name, dst, tiles, quads):
                n = 0
                for t in tiles:
                    for j in quads:
                        unit_hi_half(l, name, n, dst[:, 4 * j:4 * j + 4, t * P:(t + 1) * P])
                        n += 1

            def retention_head(l, h):
                for n in range(3):
                    i = 3 * h + n
                    act.wait_ge(kv_used, l * 12 + (i + 1 + 2))
                    act.activation(state[:, n], kv_sum[:, n], ACT.Copy, scale=GAMMA_C[h]).then_inc(state_ready, 1)
                for n in range(NT):
                    act.wait_ge(y_read, l * 16 + (4 * h + n + 1 + 2))
                    act.activation(y_sq[:], y[:, n, h * DV:(h + 1) * DV], ACT.Square,
                                   accum_out=y_ss[:, 4 * h + n:4 * h + n + 1])
                    act.drain()

            def retention_pair(l, h0):
                retention_head(l, h0)
                retention_head(l, h0 + 1)

            def head_deviations(l, pair):
                act.activation(y_std[:, 8 * pair:8 * pair + 8], y_ss[:, 8 * pair:8 * pair + 8], ACT.Sqrt,
                               bias=k("eps"), scale=1.0 / DV).then_inc(y_std_ready, 1)

            def acc_wait(l, g, t):
                if t < 3:
                    act.wait_ge(acc_ready, l * (3 * NGROUP) + (3 * g + t + 1))
                else:
                    act.wait_ge(w_used, w_done(l, LAST[NAMES[g]]))

            def read_group(l, g):
                name = NAMES[g]
                for t in range(NT):
                    if name in ("v0", "v1"):
                        half = int(name[1])
                        acc_wait(l, g, t)
                        for j in range(2):
                            h = 2 * half + j
                            last = act.activation(y[:, t, h * DV:(h + 1) * DV], ps[:, t, j * DV:(j + 1) * DV],
                                                  ACT.Copy, scale=k("vscale")[:, h:h + 1])
                        last.then_inc(acc_free, 1)
                    elif name == "u":
                        if t == 0:
                            act.wait_ge(x_saved, l * 16 + 16)
                        acc_wait(l, g, t)
                        act.activation(u[:, t], ps[:, t], ACT.Copy).then_inc(acc_free, 1)
                    elif name in ("g0", "g1"):
                        acc_wait(l, g, t)
                        act.wait_ge(gated, l * 8 + (4 * int(name[1]) + t + 1))
                        act.activation(tmp[:, t % 2], ps[:, t], ACT.Sigmoid).then_inc(gate_sig, 1)
                    elif name in ("ap0", "ap1"):
                        acc_wait(l, g, t)
                        act.activation(merged[:, int(name[2]), t], ps[:, t], ACT.Sigmoid).then_inc(acc_free, 1)
                    elif name in ("ar0", "ar1"):
                        acc_wait(l, g, t)
                        if name == "ar1":
                            act.wait_ge(merged_add, l * 8 + (t + 1))
                        act.activation(sig_ret[:, t], ps[:, t], ACT.Sigmoid).then_inc(acc_free, 1)

            def misc(l, name):
                if name == "u":
                    retention_pair(l, 0)
                    head_deviations(l, 0)
                elif name == "g0":
                    retention_pair(l, 2)
                    head_deviations(l, 1)
                elif name == "ap0":
                    transposed_hi(l, "y", yT_hi, range(NT), range(2))
                    for g in range(4):
                        unit_hi_half(l, "pw", g, ypT_hi[:, g], scale=pscale[:, g:g + 1])
                elif name == "ar1":
                    transposed_hi(l, "m0", hT_hi, range(NT), [0])
                elif name == "R1":
                    transposed_hi(l, "m1", hT_hi, range(NT), [1])

            def expert(l, e, odd, last):
                E = l * NE + e
                q0 = l * PROD + e * EXP

                def hi_e(n):
                    r = 12 * odd + n
                    base = l * (16 * RAW // RAW_SLOTS) + (e - odd) * (16 * EXP // RAW_SLOTS)
                    act.wait_ge(landed[r % RAW_SLOTS], base + 16 * ((PRE + RAW_MIX + r) // RAW_SLOTS + 1))
                    act.wait_ge(w_used, q0 + (MIX + n + 1))
                    act.activation(w_hi[:, n % W_SLOTS], raw[:, r % RAW_SLOTS], ACT.Copy).then_inc(w_hi_ready, 1)

                def sig(half):
                    act.wait_ge(w_used, q0 + (MIX + 4 * half + 4 + W_SLOTS))
                    act.activation(tmp[:, half, 0:256], ps[:, half, 0:256], ACT.Sigmoid).then_inc(act_sig, 1)

                def hidT(half):
                    act.wait_ge(hidT_ready, E * 2 + (half + 1))
                    act.activation(hidT_hi[:, 256 * half:256 * half + 256], ps[:, 6 + half, 0:256],
                                   ACT.Copy).then_inc(hidT_hi_ready, 1)

                hi_e(4)
                hi_e(5)
                sig(0)
                hi_e(6)
                hi_e(7)
                hidT(0)
                hi_e(8)
                hi_e(9)
                sig(1)
                hi_e(10)
                hi_e(11)
                hidT(1)
                if not last:
                    hi_e(12)
                    hi_e(13)
                    gathered_hi(E + 1, 1 - odd)
                    hi_e(14)
                    hi_e(15)
                act.wait_ge(w_used, q0 + (MIX + EXP + W_SLOTS))
                act.wait_ge(row_stored[odd], l * 160 + (e - odd) * 8 + 32)
                for half in range(2):
                    one = act.activation(y_out[:, odd, 512 * half:512 * half + 512], ps[:, 2 + half], ACT.Copy)
                one.then_inc(y_copied, 1)

            def gathered_hi(E, slot):
                for j in range(2):
                    act.wait_ge(xgT_ready, E * 2 + (j + 1 + 2))
                    act.activation(xgT_hi[:, slot, 512 * j:512 * j + 512], ps[:, 4 + j], ACT.Copy).then_inc(xgT_hi_ready, 1)

            apart(act)
            with act.Fori(0, DEPTH) as l:
                for q in range(W_SLOTS):
                    hi(l, q, RAW_OF_W[q])
                act.wait_ge(x_final, l * NT + NT)
                row_deviations(l, 0)
                transposed_hi(l, "h1", hT_hi, range(NT), range(2))
                for q in range(MIX):
                    for g in range(NGROUP):
                        if LAST[NAMES[g]] == q:
                            read_group(l, g)
                            misc(l, NAMES[g])
                    if q + W_SLOTS < MIX:
                        hi(l, q + W_SLOTS, RAW_OF_W[q + W_SLOTS])
                for q in range(W_SLOTS):
                    hi(l, MIX + q, RAW_MIX + q)
                act.wait_ge(x_added, l * 8 + 8)
                row_deviations(l, 1)
                transposed_hi(l, "h2", hT_hi, range(NT), range(2))
                act.wait_ge(max_off, l + 1)
                act.activation(probs[:], lg[:], ACT.Exp).then_inc(exp_done, 1)
                gathered_hi(l * NE, 0)
                apart(act)
                with act.Fori(0, NE // 2 - 1) as j:
                    expert(l, j * 2, 0, False)
                    expert(l, j * 2 + 1, 1, False)
                expert(l, NE - 2, 0, False)
                expert(l, NE - 1, 1, True)

                act.wait_ge(idx_ready, l + 1)
                before, count = overflow_blocks(act, l)
                with act.If(count > 0):
                    apart(act)
                    with act.Fori(0, count) as slot:
                        b = slot + before
                        act.wait_ge(ov_step, b * OV_STEPS + 13)
                        for half in range(2):
                            one = act.activation(o_sig[:, half], ps[:, half, 0:256], ACT.Sigmoid)
                        one.then_inc(ov_step, 1)
                act.nop()
                for t in range(NT):
                    act.wait_ge(pair_in[t % 2][0], l * 32 + 16 * (t // 2 + 1))
                    act.activation(y_pair[:, t % 2, 0], y_pair[:, t % 2, 0], ACT.Copy,
                                   scale=wts[:, t:t + 1]).then_inc(pair_scaled, 1)
            act.wait_ge(x_final, DEPTH * NT + NT)
            row_deviations(0, 0)

        @block.vector
        def _(v):
            v.sem_inc(raw_used, RAW_SLOTS)
            v.sem_inc(acc_free, 4)
            v.sem_inc(unit_free, 2)
            v.sem_inc(kv_used, 2)
            v.sem_inc(y_read, 2)
            v.sem_inc(gated, 2)
            v.wait_ge(wr_hi_ready, 1)
            v.tensor_tensor(wr_lo[:], k("wr"), wr_hi[:], ALU.subtract)
            v.memset(ov_range_f[:], 0.0)
            v.wait_ge(cond_sig, 1)
            v.drain()
            v.tensor_tensor(cond[:], cond[:], cond_raw[:], ALU.mult)
            v.drain()
            v.wait_ge(x_landed, 16)
            v.sem_inc(x_final, NT)

            def lo(l, q, r):
                v.wait_ge(w_hi_ready, l * PROD + (q + 1))
                v.tensor_tensor(w_lo[:, q % W_SLOTS], raw[:, r % RAW_SLOTS], w_hi[:, q % W_SLOTS],
                                ALU.subtract).then_inc(raw_used, 1)

            def ada_products(wait_piece, slot0):
                for j in range(ADA_PIECES):
                    wait_piece(j)
                    for i in range(2):
                        piece = raw[:, (slot0 + j) % RAW_SLOTS, 512 * i:512 * i + 512]
                        c = cond[:, 2 * j + i:2 * j + i + 1]
                        if j == 0 and i == 0:
                            one = v.tensor_scalar(ada_acc[:], piece, c, None, ALU.mult)
                        else:
                            one = v.scalar_tensor_tensor(ada_acc[:], piece, c, ada_acc[:], ALU.mult, ALU.add)
                        if i == 1:
                            one.then_inc(raw_used, 1)
                        last = v.drain()
                last.then_inc(ada_mac, 1)

            def ada_finish(a_all, scale):
                v.wait_ge(ada_sum, a_all + 1)
                v.wait_ge(ada_add_landed, (a_all + 1) * 16)
                one = v.tensor_tensor(ada_row[:], ps[0:1, 7], ada_add[:, 0], ALU.add)
                if scale:
                    v.drain()
                    one = v.scalar_tensor_tensor(ada_row[:], ada_row[:], 1.0, ada_add[:, 1], ALU.add, ALU.mult)
                one.then_inc(ada_row_ready, 1)

            for a in range(4):
                if a:
                    v.wait_ge(ada_sum, a)
                ada_products(lambda j, a=a: v.wait_ge(landed[(4 * a + j) % RAW_SLOTS], 16 * ((4 * a + j) // RAW_SLOTS + 1)),
                             4 * a)
                if a:
                    v.wait_ge(mod_stored[(a - 1) % 2], 16 * ((a - 1) // 2 + 1))
                ada_finish(a, a >= 2)

            def modulated_norm(l, which, name):
                v.wait_ge(x_std_ready, l * 2 + (which + 1))
                v.reciprocal(x_rs[:], x_std[:])
                v.drain()
                v.wait_ge(norm_rows, l * 64 + 32 * (which + 1))
                for t in range(NT):
                    if t >= 2:
                        v.wait_ge(unit_ready, unit_value(l, name, 2 * (t - 2) + 1))
                        if which == 1:
                            v.wait_ge(row_stored[t % 2], l * 160 + 16)
                    v.scalar_tensor_tensor(h_nat[:, t % 2], x[:, t], x_rs[:, t:t + 1], scale_row[:], ALU.mult, ALU.mult)
                    v.drain()
                    v.tensor_tensor(h_nat[:, t % 2], h_nat[:, t % 2], shift_row[:], ALU.add).then_inc(h_ready, 1)
                    if t >= 1:
                        for j in range(2):
                            unit_lo_half(l, name, 2 * (t - 1) + j, hT_hi, hT_lo, t - 1, j)
                for j in range(2):
                    unit_lo_half(l, name, 2 * (NT - 1) + j, hT_hi, hT_lo, NT - 1, j)

            def unit_lo_half(l, name, n, dst_hi, dst_lo, t, j):
                bank = 4 + (UNIT0[name] + n) % 2
                v.wait_ge(unit_hi, l * NSPLIT + (SPLIT0[name] + n + 1))
                where = (slice(None), slice(4 * j, 4 * j + 4), slice(t * P, (t + 1) * P))
                v.tensor_tensor(dst_lo[where], ps[:, bank].rearrange("p (a b) -> p a b", a=4), dst_hi[where],
                                ALU.subtract).then_inc(unit_free, 1)

            def acc_wait(l, g, t):
                if t < 3:
                    v.wait_ge(acc_ready, l * (3 * NGROUP) + (3 * g + t + 1))
                else:
                    v.wait_ge(w_used, w_done(l, LAST[NAMES[g]]))

            def read_group(l, g):
                name = NAMES[g]
                for t in range(NT):
                    if name in ("q", "k"):
                        dst = (q_rot if name == "q" else k_rot)[:, t]
                        if name == "q" and t == 0:
                            v.wait_ge(rope_landed, l * 16 + 16)
                        acc_wait(l, g, t)
                        a4 = ps[:, t].rearrange("p (h d) -> p h d", h=HEADS)
                        b4 = tmp[:, t % 2].rearrange("p (h d) -> p h d", h=HEADS)
                        cos = rope[:, 0, t].unsqueeze(1)
                        sin = rope[:, 1, t].unsqueeze(1)
                        v.tensor_tensor(dst.rearrange("p (h d) -> p h d", h=HEADS), a4, cos.broadcast_to([P, HEADS, DK]), ALU.mult)
                        v.tensor_tensor(b4[:, :, 0:64], a4[:, :, 64:128], sin[:, :, 0:64].broadcast_to([P, HEADS, 64]), ALU.mult)
                        v.tensor_tensor(b4[:, :, 64:128], a4[:, :, 0:64], sin[:, :, 64:128].broadcast_to([P, HEADS, 64]),
                                        ALU.mult).then_inc(acc_free, 1)
                        v.drain()
                        v.tensor_tensor(dst, dst, tmp[:, t % 2], ALU.add).then_inc(rot_done, 1)
                    elif name in ("g0", "g1"):
                        pair = int(name[1])
                        acc_wait(l, g, t)
                        v.wait_ge(gate_sig, l * 8 + (4 * pair + t + 1))
                        v.tensor_tensor(tmp[:, t % 2], tmp[:, t % 2], ps[:, t], ALU.mult).then_inc(acc_free, 1)
                        v.drain()
                        for j in range(2):
                            h = 2 * pair + j
                            yh = y[:, t, h * DV:(h + 1) * DV]
                            one = v.scalar_tensor_tensor(yh, yh, y_rs[:, 4 * h + t:4 * h + t + 1],
                                                         tmp[:, t % 2, j * DV:(j + 1) * DV], ALU.mult, ALU.mult)
                        one.then_inc(gated, 1)
                    elif name in ("P0", "P1"):
                        acc_wait(l, g, t)
                        v.wait_ge(acc_free, acc_value(l, g - 1, t))
                        m = merged[:, int(name[1]), t]
                        v.tensor_tensor(m, m, ps[:, t], ALU.mult).then_inc(acc_free, 1)
                    elif name in ("R0", "R1"):
                        acc_wait(l, g, t)
                        v.wait_ge(acc_free, acc_value(l, g - 1, t))
                        m = merged[:, int(name[1]), t]
                        v.tensor_tensor(sig_ret[:, t], sig_ret[:, t], ps[:, t], ALU.mult).then_inc(acc_free, 1)
                        v.drain()
                        v.tensor_tensor(m, m, sig_ret[:, t], ALU.add).then_inc(merged_add, 1)
                    elif name in ("O0", "O1"):
                        half = int(name[1])
                        if half == 0 and t == 0:
                            v.wait_ge(x_back, l * 16 + 16)
                            v.wait_ge(gate_landed, l * 32 + 16)
                        acc_wait(l, g, t)
                        cols = slice(512 * half, 512 * half + 512)
                        v.tensor_tensor(tmp[:, t % 2], ps[:, t], gate_row[:, cols], ALU.mult).then_inc(acc_free, 1)
                        v.drain()
                        v.tensor_tensor(x[:, t, cols], x[:, t, cols], tmp[:, t % 2], ALU.add).then_inc(x_added, 1)

            def retention_pair(l, h0):
                def mask(h):
                    v.wait_ge(score_ready, l * HEADS + (h + 1))
                    v.tensor_tensor(scores[:, h % 2].rearrange("p (n c) -> p n c", n=NT),
                                    ps[:, 4 + h % 2].rearrange("p (n c) -> p n c", n=NT),
                                    k("causal").unsqueeze(1).broadcast_to([P, NT, P]), ALU.mult).then_inc(score_masked, 1)

                def kv(h):
                    for n in range(3):
                        i = 3 * h + n
                        if n != 1:
                            v.wait_ge(kv_ready, l * 8 + (2 * h + n // 2 + 1))
                        v.wait_ge(state_ready, l * 12 + (i + 1))
                        if n == 0:
                            v.tensor_copy(kv_sum[:, 0], ps[:, 6, 0:DV]).then_inc(kv_used, 1)
                        else:
                            src = ps[:, 6, DV:2 * DV] if n == 1 else ps[:, 0, 0:DV]
                            v.scalar_tensor_tensor(kv_sum[:, n], kv_sum[:, n - 1], GAMMA_C[h], src, ALU.mult,
                                                   ALU.add).then_inc(kv_used, 1)
                        v.drain()

                def y_tiles(h, part, bank):
                    v.wait_ge(y_ready, l * 8 + (2 * h + part + 1))
                    for n in (2 * part, 2 * part + 1):
                        v.tensor_scalar(y[:, n, h * DV:(h + 1) * DV], ps[:, bank, DV * (n % 2):DV * (n % 2) + DV],
                                        k("xi")[:, h:h + 1], None, ALU.mult).then_inc(y_read, 1)

                mask(h0)
                kv(h0)
                mask(h0 + 1)
                y_tiles(h0, 0, 1)
                y_tiles(h0, 1, 2)
                kv(h0 + 1)
                y_tiles(h0 + 1, 0, 3)
                y_tiles(h0 + 1, 1, 1)

            def head_scales(l, pair):
                v.wait_ge(y_std_ready, l * 2 + (pair + 1))
                v.reciprocal(y_rs[:, 8 * pair:8 * pair + 8], y_std[:, 8 * pair:8 * pair + 8])
                v.drain()

            def misc(l, name):
                if name == "v0":
                    for which, dst in (("q", qT), ("k", kT)):
                        for t in range(NT):
                            v.wait_ge(unit_ready, unit_value(l, which, t))
                            v.tensor_copy(dst[:, :, t * P:(t + 1) * P],
                                          ps[:, 4 + (UNIT0[which] + t) % 2].rearrange("p (a b) -> p a b", a=HEADS)
                                          ).then_inc(unit_free, 1)
                elif name == "u":
                    retention_pair(l, 0)
                    head_scales(l, 0)
                elif name == "g0":
                    for g in range(4):
                        v.wait_ge(unit_ready, unit_value(l, "mix", g))
                        v.tensor_copy(mixT[:, g], ps[:, 4 + (UNIT0["mix"] + g) % 2]).then_inc(unit_free, 1)
                    retention_pair(l, 2)
                    head_scales(l, 1)
                elif name == "ap0":
                    for t in range(NT):
                        for j in range(2):
                            unit_lo_half(l, "y", 2 * t + j, yT_hi, yT_lo, t, j)
                    for g in range(4):
                        v.wait_ge(unit_hi, l * NSPLIT + (SPLIT0["pw"] + g + 1))
                        v.scalar_tensor_tensor(ypT_lo[:, g], ps[:, 4 + (UNIT0["pw"] + g) % 2], pscale[:, g:g + 1],
                                               ypT_hi[:, g], ALU.mult, ALU.subtract).then_inc(unit_free, 1)
                elif name == "ar1":
                    for t in range(NT):
                        unit_lo_half(l, "m0", t, hT_hi, hT_lo, t, 0)
                elif name == "R1":
                    for t in range(NT):
                        unit_lo_half(l, "m1", t, hT_hi, hT_lo, t, 1)

            def ada_step(l, g):
                if 1 <= g <= NADA:
                    a = g - 1
                    v.wait_ge(mod_stored[(a + 1) % 2], l * (8 * NADA) + 16 * ((3 + a) // 2 + 1))
                    ada_finish(l * NADA + (4 + a), a in (4, 5, 10, 11))
                if g < NADA:
                    r0 = RAW_OF_ADA[(g, 0)]
                    ada_products(lambda j: v.wait_ge(landed[(r0 + j) % RAW_SLOTS], land_value(l, r0 + j)), r0)

            def route_tokens(l):
                lg3 = lg[:].rearrange("p (t e) -> p t e", e=NE)
                pr3 = probs[:].rearrange("p (t e) -> p t e", e=NE)
                pr4 = probs[:].rearrange("p (s e) -> p s e", e=4)
                rt3 = rt[:].rearrange("p (t e) -> p t e", e=NE)
                rt4 = rt[:].rearrange("p (s e) -> p s e", e=4)
                s43 = s4[:].rearrange("p (t g) -> p t g", g=NG)
                s4b3 = s4b[:].rearrange("p (t g) -> p t g", g=NG)
                pairs3 = pairs[:].rearrange("p (a b) -> p a b", b=6)
                pos3 = pos[:].rearrange("p (t e) -> p t e", e=NE)
                ch3 = chosen[:].rearrange("p (t e) -> p t e", e=NE)
                hots = [hot1[:].rearrange("p (t e) -> p t e", e=NE), hot2[:].rearrange("p (t e) -> p t e", e=NE)]

                def wide(a, n=NE):
                    return a.unsqueeze(2).broadcast_to([P, NT, n])

                def tt(dst, a, b, op):
                    one = v.tensor_tensor(dst, a, b, op)
                    v.drain()
                    return one

                def first_largest(dst3, src3, biggest, n, rev):
                    tt(dst3, src3, wide(biggest, n), ALU.is_equal)
                    tt(dst3, dst3, rev.unsqueeze(1).broadcast_to([P, NT, n]), ALU.mult)
                    v.tensor_reduce(r1[:], dst3, AX, ALU.max)
                    v.drain()
                    tt(dst3, dst3, wide(r1[:], n), ALU.is_equal)

                v.wait_ge(logits_ready, l + 1)
                tt(lg3, ps[:, 6, 0:64].rearrange("p (t e) -> p t e", e=NE),
                   k("br").unsqueeze(1).broadcast_to([P, NT, NE]), ALU.add)
                v.tensor_reduce(r1[:], lg3, AX, ALU.max)
                v.drain()
                v.tensor_tensor(lg3, lg3, wide(r1[:]), ALU.subtract).then_inc(max_off, 1)
                v.wait_ge(exp_done, l + 1)
                v.tensor_reduce(r1[:], pr3, AX, ALU.add)
                v.drain()
                v.reciprocal(top[:, 0:4], r1[:])
                v.drain()
                tt(pr3, pr3, wide(top[:, 0:4]), ALU.mult)
                v.tensor_tensor(pairs3[:, :, 0:3], pr4[:, :, 0:3], pr4[:, :, 1:4], ALU.add)
                v.tensor_tensor(pairs3[:, :, 3:5], pr4[:, :, 0:2], pr4[:, :, 2:4], ALU.add)
                tt(pairs3[:, :, 5:6], pr4[:, :, 0:1], pr4[:, :, 3:4], ALU.add)
                v.tensor_reduce(s4[:], pairs3, AX, ALU.max)
                v.drain()
                v.tensor_reduce(top[:, 0:4], s43, AX, ALU.max)
                v.drain()
                first_largest(s4b3, s43, top[:, 0:4], NG, k("rev4"))
                group = s4b[:].unsqueeze(2).broadcast_to([P, NT * NG, 4])
                tt(rt4, pr4, group, ALU.mult)
                v.tensor_scalar(s4[:], s4b[:], -1.0, None, ALU.add)
                v.drain()
                tt(rt4, rt4, s4[:].unsqueeze(2).broadcast_to([P, NT * NG, 4]), ALU.add)
                v.tensor_reduce(top[:, 0:4], rt3, AX, ALU.max)
                v.drain()
                first_largest(hots[0], rt3, top[:, 0:4], NE, k("rev16"))
                v.scalar_tensor_tensor(rt[:], hot1[:], -4.0, rt[:], ALU.mult, ALU.add)
                v.drain()
                v.tensor_reduce(top[:, 4:8], rt3, AX, ALU.max)
                v.drain()
                first_largest(hots[1], rt3, top[:, 4:8], NE, k("rev16"))
                v.tensor_tensor(chosen[:], hot1[:], hot2[:], ALU.add).then_inc(chosen_ready, 1)
                v.tensor_tensor(r1[:], top[:, 0:4], top[:, 4:8], ALU.add)
                v.drain()
                v.reciprocal(r1[:], r1[:])
                v.drain()
                v.tensor_tensor(wts[:, 0:4], top[:, 0:4], r1[:], ALU.mult)
                v.tensor_tensor(wts[:, 4:8], top[:, 4:8], r1[:], ALU.mult)
                for j in range(2):
                    v.tensor_tensor(hotid[:, 64 * j:64 * j + 64].rearrange("p (t e) -> p t e", e=NE), hots[j],
                                    wide(k("tokid")), ALU.mult)

                v.wait_ge(pos_ready, l + 1)
                v.tensor_copy(pos[:], ps[:, 7, 0:64])
                v.tensor_scalar(ovn[:], ps[:, 7, 64:80], float(CAP), None, ALU.is_gt)
                v.drain()
                for level in range(2, LEVELS):
                    v.scalar_tensor_tensor(ovn[:], ps[:, 7, 64:80], float(level * CAP), ovn[:], ALU.is_gt, ALU.add)
                    v.drain()
                for j in range(2):
                    tt(rt3, hots[j], pos3, ALU.mult)
                    v.tensor_reduce(posk[:, 4 * j:4 * j + 4], rt3, AX, ALU.add)
                    v.drain()
                for j in range(2):
                    for t in range(NT):
                        one = v.tensor_scalar(hot[:, j, t], k("iota"), posk[:, 4 * j + t:4 * j + t + 1], None, ALU.is_equal)
                one.then_inc(hot_ready, 1)

                v.memset(ovc[:, 0:16], 0.0)
                v.memset(ovd[:, 0:16], 0.0)
                v.tensor_copy(ovc[:, 16:32], ovn[:])
                v.drain()
                a, b = ovc, ovd
                for s in (1, 2, 4, 8):
                    tt(b[:, 16:32], a[:, 16:32], a[:, 16 - s:32 - s], ALU.add)
                    a, b = b, a
                tt(ov_range_f[:, 0:1], ov_range_f[:, 0:1], ov_range_f[:, 1:2], ALU.add)
                tt(ovd[:, 16:32], ovc[:, 16:32], ovn[:], ALU.subtract)
                v.tensor_copy(ov_range_f[:, 1:2], ovc[:, 31:32])
                v.drain()
                v.tensor_copy(ov_range[:], ov_range_f[:])
                t3 = ovt[:].rearrange("p (b e) -> p b e", e=NE)
                t23 = ovt2[:].rearrange("p (b e) -> p b e", e=NE)
                block_id = k("blockid").unsqueeze(2).broadcast_to([P, NOV, NE])
                v.tensor_tensor(t3, ovd[:, 16:32].unsqueeze(1).broadcast_to([P, NOV, NE]), block_id, ALU.is_le)
                tt(t23, ovc[:, 16:32].unsqueeze(1).broadcast_to([P, NOV, NE]), block_id, ALU.is_gt)
                tt(t3, t3, t23, ALU.mult)
                tt(t3, t3, k("eid").unsqueeze(1).broadcast_to([P, NOV, NE]), ALU.mult)
                v.tensor_reduce(ovt2[:, 0:NOV], t3, AX, ALU.add)
                v.drain()
                v.tensor_copy(ov_expert[:], ovt2[:, 0:NOV])
                v.tensor_scalar(ovd[:, 16:32], ovd[:, 16:32], float(NE - 1), float(CAP), ALU.add, ALU.mult)
                v.drain()
                tt(ovd[:, 16:32], ovd[:, 16:32], k("ecap"), ALU.subtract)
                v.tensor_scalar(rt[:], pos[:], float(CAP), None, ALU.is_ge)
                v.drain()
                tt(rt3, rt3, ovd[:, 16:32].unsqueeze(1).broadcast_to([P, NT, NE]), ALU.mult)
                tt(rt3, rt3, k("ecap").unsqueeze(1).broadcast_to([P, NT, NE]), ALU.add)
                tt(pos3, rt3, pos3, ALU.add)
                for j in range(2):
                    tt(rt3, hots[j], pos3, ALU.mult)
                    v.tensor_reduce(slotf[:, 4 * j:4 * j + 4], rt3, AX, ALU.add)
                    v.drain()
                v.tensor_copy(slot_i[:], slotf[:])
                v.memset(ov_base[:], float(NE * CAP))
                v.drain()
                v.wait_ge(idx_sum, l + 1)
                v.tensor_copy(idx[:], ps[:, 6, 64:80]).then_inc(idx_ready, 1)

            def gathered_lo(E, slot):
                for j in range(2):
                    v.wait_ge(xgT_hi_ready, E * 2 + (j + 1))
                    cols = slice(512 * j, 512 * j + 512)
                    v.tensor_tensor(xgT_lo[:, slot, cols], ps[:, 4 + j], xgT_hi[:, slot, cols],
                                    ALU.subtract).then_inc(xgT_lo_ready, 1)

            def expert(l, e, odd, last):
                E = l * NE + e
                q0 = l * PROD + e * EXP

                def lo_e(n):
                    r = 12 * odd + n
                    v.wait_ge(w_hi_ready, q0 + (MIX + n + 1))
                    v.tensor_tensor(w_lo[:, n % W_SLOTS], raw[:, r % RAW_SLOTS], w_hi[:, n % W_SLOTS],
                                    ALU.subtract).then_inc(raw_used, 1)

                def hidden(half):
                    v.wait_ge(act_sig, E * 2 + (half + 1))
                    s = tmp[:, half, 0:256]
                    v.tensor_tensor(s, s, ps[:, half, 0:256], ALU.mult)
                    v.drain()
                    v.tensor_tensor(hid[:, 256 * half:256 * half + 256], s, ps[:, half, 256:512],
                                    ALU.mult).then_inc(hid_ready, 1)

                def hidT(half):
                    v.wait_ge(hidT_hi_ready, E * 2 + (half + 1))
                    cols = slice(256 * half, 256 * half + 256)
                    v.tensor_tensor(hidT_lo[:, cols], ps[:, 6 + half, 0:256], hidT_hi[:, cols],
                                    ALU.subtract).then_inc(hidT_lo_ready, 1)

                lo_e(4)
                lo_e(5)
                hidden(0)
                lo_e(6)
                lo_e(7)
                hidT(0)
                lo_e(8)
                lo_e(9)
                hidden(1)
                lo_e(10)
                lo_e(11)
                hidT(1)
                if not last:
                    lo_e(12)
                    lo_e(13)
                    gathered_lo(E + 1, 1 - odd)
                    lo_e(14)
                    lo_e(15)

            apart(v)
            with v.Fori(0, DEPTH) as l:
                for q in range(W_SLOTS):
                    lo(l, q, RAW_OF_W[q])
                modulated_norm(l, 0, "h1")
                for q in range(MIX):
                    for g in range(NGROUP):
                        if LAST[NAMES[g]] == q:
                            read_group(l, g)
                            misc(l, NAMES[g])
                            ada_step(l, g)
                    if q + W_SLOTS < MIX:
                        lo(l, q + W_SLOTS, RAW_OF_W[q + W_SLOTS])
                for q in range(W_SLOTS):
                    lo(l, MIX + q, RAW_MIX + q)
                modulated_norm(l, 1, "h2")
                route_tokens(l)
                gathered_lo(l * NE, 0)
                apart(v)
                with v.Fori(0, NE // 2 - 1) as j:
                    expert(l, j * 2, 0, False)
                    expert(l, j * 2 + 1, 1, False)
                expert(l, NE - 2, 0, False)
                expert(l, NE - 1, 1, True)

                before, count = overflow_blocks(v, l)
                with v.If(count > 0):
                    v.wait_ge(w_used, l * PROD + (PROD + W_SLOTS))
                    apart(v)
                    with v.Fori(0, count) as slot:
                        b = slot + before
                        for j in range(2):
                            for t in range(NT):
                                one = v.tensor_scalar(o_hot[:, 4 * j + t], k("iota"), ov_base[:, 0:1],
                                                      slotf[:, 4 * j + t:4 * j + t + 1], ALU.add, ALU.is_equal)
                        v.drain()
                        v.tensor_scalar(ov_base[:], ov_base[:], float(CAP), None, ALU.add).then_inc(ov_step, 1)
                        v.wait_ge(ov_step, b * OV_STEPS + 2)
                        v.tensor_copy(o_idx[:], ps[:, 6, 0:1]).then_inc(ov_step, 1)
                        v.wait_ge(ov_step, b * OV_STEPS + 4)
                        v.tensor_copy(o_xT[:, 0:4], ps[:, 4].rearrange("p (a b) -> p a b", a=4))
                        v.tensor_copy(o_xT[:, 4:8], ps[:, 5].rearrange("p (a b) -> p a b", a=4)).then_inc(ov_step, 1)
                        v.wait_ge(ov_step, b * OV_STEPS + 14)
                        for half in range(2):
                            v.tensor_tensor(o_sig[:, half], o_sig[:, half], ps[:, half, 0:256], ALU.mult)
                        v.drain()
                        for half in range(2):
                            one = v.tensor_tensor(o_hid[:, 256 * half:256 * half + 256], o_sig[:, half],
                                                  ps[:, half, 256:512], ALU.mult)
                        one.then_inc(ov_step, 1)
                        v.wait_ge(ov_step, b * OV_STEPS + 16)
                        v.tensor_copy(o_hidT[:], ps[:, 6].rearrange("p (a b) -> p a b", a=4)).then_inc(ov_step, 1)
                        v.wait_ge(ov_step, b * OV_STEPS + 21)
                        v.tensor_copy(o_y[:, 0:512], ps[:, 2])
                        v.tensor_copy(o_y[:, 512:1024], ps[:, 3]).then_inc(ov_step, 1)
                        v.drain()
                v.nop()

                v.wait_ge(gate_landed, l * 32 + 32)
                for t in range(NT):
                    v.wait_ge(pair_in[t % 2][1], l * 32 + 16 * (t // 2 + 1))
                    v.wait_ge(pair_scaled, l * NT + (t + 1))
                    s = y_pair[:, t % 2, 0]
                    v.scalar_tensor_tensor(s, y_pair[:, t % 2, 1], wts[:, 4 + t:5 + t], s, ALU.mult, ALU.add)
                    v.drain()
                    v.tensor_tensor(s, s, gate_row[:], ALU.mult)
                    v.drain()
                    v.tensor_tensor(x[:, t], x[:, t], s, ALU.add).then_inc(x_final, 1)

            v.wait_ge(x_std_ready, DEPTH * 2 + 1)
            v.reciprocal(x_rs[:], x_std[:])
            v.drain()
            v.wait_ge(norm_rows, DEPTH * 64 + 16)
            for t in range(NT):
                v.scalar_tensor_tensor(x[:, t], x[:, t], x_rs[:, t:t + 1], scale_row[:], ALU.mult,
                                       ALU.mult).then_inc(norm_done, 1)

        @block.tensor
        def _(pe):
            pe.sem_inc(w_used, W_SLOTS)
            pe.sem_inc(xgT_ready, 2)
            pe.wait_ge(consts_landed, 16)

            def three_passes(dst, a_hi, a_lo, b_hi, b_lo, start, stop):
                pe.matmul(dst, a_lo, b_hi, start=start, stop=False)
                pe.matmul(dst, a_hi, b_lo, start=False, stop=False)
                return pe.matmul(dst, a_hi, b_hi, start=False, stop=stop)

            def group(l, g):
                name, n = GROUPS[g]
                if name in ("g0", "g1"):
                    h0 = 2 * int(name[1])
                    pe.wait_ge(kv_used, l * 12 + (3 * h0 + 6 + 2))
                    pe.wait_ge(y_read, l * 16 + (4 * h0 + 8 + 2))
                left_hi, left_lo = {"P": (ypT_hi, ypT_lo), "R": (yT_hi, yT_lo)}.get(name[0], (hT_hi, hT_lo))
                for j in range(n):
                    q = FIRST[name] + j
                    s = q % W_SLOTS
                    pe.wait_ge(raw_used, raw_value(l, RAW_OF_W[q]))
                    for t in range(NT):
                        if j == 0:
                            pe.wait_ge(acc_free, l * (4 * NGROUP) + (4 * g + t + 1))
                        for i in range(2):
                            cols = slice(t * P, (t + 1) * P)
                            w_cols = slice(512 * i, 512 * i + 512)
                            mm = three_passes(ps[:, t], left_hi[:, 2 * j + i, cols], left_lo[:, 2 * j + i, cols],
                                              w_hi[:, s, w_cols], w_lo[:, s, w_cols],
                                              j == 0 and i == 0, j == n - 1 and i == 1)
                        if j == n - 1 and t < 3:
                            mm.then_inc(acc_ready, 1)
                    mm.then_inc(w_used, 1)

            def unit(l, name, n):
                pe.wait_ge(unit_free, l * NUNIT + (UNIT0[name] + n + 1))
                return ps[:, 4 + (UNIT0[name] + n) % 2]

            def units_done(l, name):
                n = UNITS[name]
                pe.wait_ge(unit_free, l * NUNIT + (UNIT0[name] + n + 2))

            def transposes(l, name, n, src):
                bank = unit(l, name, n)
                for i in range(4):
                    one = pe.transpose(bank[:, i * P:(i + 1) * P], src[:, i * P:(i + 1) * P], ident)
                one.then_inc(unit_ready, 1)

            def norm_transposes(l, which, name):
                for t in range(NT):
                    pe.wait_ge(h_ready, l * 8 + (4 * which + t + 1))
                    for j in range(2):
                        transposes(l, name, 2 * t + j, h_nat[:, t % 2, 512 * j:512 * j + 512])
                units_done(l, name)

            def retention_pair(l, h0):
                def score(h):
                    for n in range(NT):
                        cols = slice(n * P, (n + 1) * P)
                        one = pe.matmul(ps[:, 4 + h % 2, cols], kT[:, h, cols], qT[:, h, cols], start=True, stop=True)
                    one.then_inc(score_ready, 1)

                def kv(h):
                    pe.wait_ge(kv_used, l * 12 + (3 * h + 2))
                    for n in range(2):
                        one = pe.matmul(ps[:, 6, DV * n:DV * n + DV], k_rot[:, n, h * DK:(h + 1) * DK],
                                        y[:, n, h * DV:(h + 1) * DV], start=True, stop=True)
                    one.then_inc(kv_ready, 1)
                    pe.matmul(ps[:, 0, 0:DV], k_rot[:, 2, h * DK:(h + 1) * DK], y[:, 2, h * DV:(h + 1) * DV],
                              start=True, stop=True).then_inc(kv_ready, 1)

                def y_tiles(h, part, bank):
                    if part == 0:
                        pe.wait_ge(score_masked, l * HEADS + (h + 1))
                    for n in (2 * part, 2 * part + 1):
                        dst = ps[:, bank, DV * (n % 2):DV * (n % 2) + DV]
                        one = pe.matmul(dst, scores[:, h % 2, n * P:(n + 1) * P], y[:, n, h * DV:(h + 1) * DV],
                                        start=True, stop=n == 0)
                        if n:
                            pe.wait_ge(state_ready, l * 12 + (3 * h + n + 3))
                            one = pe.matmul(dst, qT[:, h, n * P:(n + 1) * P], state[:, n - 1], start=False, stop=True)
                    one.then_inc(y_ready, 1)

                score(h0)
                score(h0 + 1)
                pe.wait_ge(acc_free, acc_value(l, NAMES.index("u" if h0 == 0 else "g0"), NT - 1))
                kv(h0)
                y_tiles(h0, 0, 1)
                y_tiles(h0, 1, 2)
                kv(h0 + 1)
                y_tiles(h0 + 1, 0, 3)
                pe.wait_ge(y_read, l * 16 + (4 * h0 + 2 + 2))
                y_tiles(h0 + 1, 1, 1)

            def ada_reduce(a_all):
                pe.wait_ge(ada_mac, a_all + 1)
                if not isinstance(a_all, int) or a_all:
                    pe.wait_ge(ada_row_ready, a_all)
                pe.matmul(ps[0:1, 7], k("ones")[:, 0:1], ada_acc[:], start=True, stop=True).then_inc(ada_sum, 1)

            def misc(l, name):
                if name == "v0":
                    pe.wait_ge(rot_done, l * 8 + 8)
                    for which, src in (("q", q_rot), ("k", k_rot)):
                        for t in range(NT):
                            transposes(l, which, t, src[:, t])
                    units_done(l, "k")
                elif name == "u":
                    retention_pair(l, 0)
                elif name == "g0":
                    pe.wait_ge(score_masked, l * HEADS + 2)
                    for g in range(4):
                        bank = unit(l, "mix", g)
                        for t in range(NT):
                            src = u[:, t, g * P:(g + 1) * P]
                            if t == 0:
                                pe.matmul(bank[:, 0:16], src, k("diag0")[:, 16 * g:16 * g + 16], start=True, stop=True)
                                one = pe.matmul(bank[:, 16:P], src, k("diag")[:, g * P + 16:(g + 1) * P], start=True, stop=True)
                            else:
                                pe.matmul(bank[:, t * P:(t + 1) * P], src, k("diag")[:, g * P:(g + 1) * P],
                                          start=True, stop=False)
                                one = pe.matmul(bank[:, t * P:t * P + 16], u[:, t - 1, g * P:(g + 1) * P],
                                                k("off")[:, 16 * g:16 * g + 16], start=False, stop=True)
                        one.then_inc(unit_ready, 1)
                    units_done(l, "mix")
                    retention_pair(l, 2)
                elif name == "ap0":
                    pe.wait_ge(gated, l * 8 + (8 + 2))
                    for t in range(NT):
                        for j in range(2):
                            transposes(l, "y", 2 * t + j, y[:, t, 512 * j:512 * j + 512])
                    pe.wait_ge(pw_landed, l * 32 + 32)
                    for g in range(4):
                        bank = unit(l, "pw", g)
                        pe.matmul(bank, pw[:, g], mixT[:, g], start=True, stop=True).then_inc(unit_ready, 1)
                    units_done(l, "pw")
                elif name == "ar1":
                    pe.wait_ge(merged_add, l * 8 + 4)
                    for t in range(NT):
                        transposes(l, "m0", t, merged[:, 0, t])
                elif name == "R1":
                    pe.wait_ge(merged_add, l * 8 + 8)
                    for t in range(NT):
                        transposes(l, "m1", t, merged[:, 1, t])
                    units_done(l, "m1")

            def gathered_transposes(E, slot):
                pe.wait_ge(gathered[slot], (E - slot) * 8 + 16)
                for j in range(2):
                    for i in range(4):
                        c = (4 * j + i) * P
                        one = pe.transpose(ps[:, 4 + j, i * P:(i + 1) * P], xg[:, slot, c:c + P], ident)
                    one.then_inc(xgT_ready, 1)

            def expert(l, e, odd, last):
                E = l * NE + e
                q0 = l * PROD + e * EXP
                r0 = l * RAW + e * EXP

                def halves_ready(n):
                    pe.wait_ge(raw_used, r0 + (PRE + RAW_MIX + n + 1 + RAW_SLOTS))

                def gate_up(n):
                    half, j = n // 4, n % 4
                    halves_ready(n)
                    if j % 2 == 0:
                        pe.wait_ge(xgT_lo_ready, E * 2 + (j // 2 + 1))
                    for i in range(2):
                        a = slice((2 * j + i) * P, (2 * j + i + 1) * P)
                        b = slice(512 * i, 512 * i + 512)
                        mm = three_passes(ps[:, half], xgT_hi[:, odd, a], xgT_lo[:, odd, a], w_hi[:, n % W_SLOTS, b],
                                          w_lo[:, n % W_SLOTS, b], j == 0 and i == 0, j == 3 and i == 1)
                    mm.then_inc(w_used, 1)

                def down(n):
                    j = n - 8
                    halves_ready(n)
                    if j == 0:
                        pe.wait_ge(y_copied, E + 1)
                    if j % 2 == 0:
                        pe.wait_ge(hidT_lo_ready, E * 2 + (j // 2 + 1))
                    for i in range(2):
                        a = slice(j * P, (j + 1) * P)
                        b = slice(512 * i, 512 * i + 512)
                        mm = three_passes(ps[:, 2 + i], hidT_hi[:, a], hidT_lo[:, a], w_hi[:, n % W_SLOTS, b],
                                          w_lo[:, n % W_SLOTS, b], j == 0, j == 3)
                    mm.then_inc(w_used, 1)

                def hidden_transposes(half):
                    pe.wait_ge(hid_ready, E * 2 + (half + 1))
                    for i in range(2):
                        c = 256 * half + i * P
                        one = pe.transpose(ps[:, 6 + half, i * P:(i + 1) * P], hid[:, c:c + P], ident)
                    one.then_inc(hidT_ready, 1)

                for n in range(6):
                    gate_up(n)
                hidden_transposes(0)
                gate_up(6)
                gate_up(7)
                down(8)
                down(9)
                hidden_transposes(1)
                if not last:
                    gathered_transposes(E + 1, 1 - odd)
                down(10)
                down(11)

            for a in range(4):
                ada_reduce(a)

            apart(pe)
            with pe.Fori(0, DEPTH) as l:
                norm_transposes(l, 0, "h1")
                pe.wait_ge(y_copied, l * NE + 1)
                for g in range(NGROUP):
                    group(l, g)
                    misc(l, NAMES[g])
                    if 1 <= g <= NADA:
                        ada_reduce(l * NADA + (4 + g - 1))
                norm_transposes(l, 1, "h2")

                for t in range(NT):
                    for i in range(8):
                        cols = slice(t * P, (t + 1) * P)
                        e = slice(NE * i, NE * i + NE)
                        mm = three_passes(ps[:, 6, NE * t:NE * t + NE], hT_hi[:, i, cols], hT_lo[:, i, cols],
                                          wr_hi[:, e], wr_lo[:, e], i == 0, i == 7)
                mm.then_inc(logits_ready, 1)
                pe.wait_ge(chosen_ready, l + 1)
                pe.wait_ge(ada_row_ready, l * NADA + (4 + NADA))
                for t in range(NT):
                    for s in range(t + 1):
                        pe.matmul(ps[:, 7, NE * t:NE * t + NE], k("ones") if s < t else k("before"),
                                  chosen[:, NE * s:NE * s + NE], start=s == 0, stop=s == t)
                for s in range(NT):
                    one = pe.matmul(ps[:, 7, 64:80], k("ones"), chosen[:, NE * s:NE * s + NE], start=s == 0, stop=s == NT - 1)
                one.then_inc(pos_ready, 1)
                pe.wait_ge(hot_ready, l + 1)
                for j in range(2):
                    for t in range(NT):
                        one = pe.matmul(ps[:, 6, 64:80], hot[:, j, t], hotid[:, 64 * j + NE * t:64 * j + NE * t + NE],
                                        start=j == 0 and t == 0, stop=j == 1 and t == NT - 1)
                one.then_inc(idx_sum, 1)

                pe.wait_ge(acc_free, acc_value(l, NGROUP - 1, NT - 1))
                gathered_transposes(l * NE, 0)
                apart(pe)
                with pe.Fori(0, NE // 2 - 1) as j:
                    expert(l, j * 2, 0, False)
                    expert(l, j * 2 + 1, 1, False)
                expert(l, NE - 2, 0, False)
                expert(l, NE - 1, 1, True)

                before, count = overflow_blocks(pe, l)
                with pe.If(count > 0):
                    pe.wait_ge(y_copied, l * NE + (NE + 1))
                    apart(pe)
                    with pe.Fori(0, count) as slot:
                        b = slot + before
                        pe.wait_ge(ov_step, b * OV_STEPS + 1)
                        for n in range(8):
                            one = pe.matmul(ps[:, 6, 0:1], o_hot[:, n], k("tokid")[:, n % NT:n % NT + 1], start=n == 0, stop=n == 7)
                        one.then_inc(ov_step, 1)
                        pe.wait_ge(ov_x, b * 16 + 16)
                        pe.wait_ge(ov_step, b * OV_STEPS + 3)
                        for i in range(8):
                            one = pe.transpose(ps[:, 4 + i // 4, (i % 4) * P:(i % 4 + 1) * P], o_x[:, i * P:(i + 1) * P], ident)
                        one.then_inc(ov_step, 1)
                        pe.wait_ge(ov_step, b * OV_STEPS + 5)
                        for n in range(EXP):
                            if n == 8:
                                pe.wait_ge(ov_step, b * OV_STEPS + 15)
                                for i in range(4):
                                    one = pe.transpose(ps[:, 6, i * P:(i + 1) * P], o_hid[:, i * P:(i + 1) * P], ident)
                                one.then_inc(ov_step, 1)
                                pe.wait_ge(ov_step, b * OV_STEPS + 17)
                            pe.wait_ge(ov_w, b * (16 * EXP) + (16 * n + 16))
                            for i in range(2):
                                piece = o_w[:, 512 * i:512 * i + 512]
                                if n < 8:
                                    mm = pe.matmul(ps[:, n // 4], o_xT[:, 2 * (n % 4) + i], piece,
                                                   start=n % 4 == 0 and i == 0, stop=n % 4 == 3 and i == 1)
                                else:
                                    mm = pe.matmul(ps[:, 2 + i], o_hidT[:, n - 8], piece, start=n == 8, stop=n == 11)
                            mm.then_inc(ov_step, 1)
                pe.nop()

        @block.gpsimd
        def _(pool):
            pool.dma_start(const[:], consts).then_inc(consts_landed, 16)
            pool.dma_start(cond_raw[:], c_in).then_inc(c_landed, 16)
            pool.dma_start(x[:].rearrange("p t d -> p (t d)"), x_in).then_inc(x_landed, 16)

            def add_load(a_all):
                pool.dma_start(ada_add[:].rearrange("p a n -> p (a n)"), ada_rows[bass.ds(a_all, 1)]).then_inc(ada_add_landed, 16)

            def mod_store(a_all, parity):
                pool.wait_ge(ada_row_ready, a_all + 1)
                apart(pool)
                pool.dma_start(mod[bass.ds(a_all, 1)], ada_row[:]).then_inc(mod_stored[parity], 16)

            for a in range(4):
                if a:
                    pool.wait_ge(ada_row_ready, a)
                apart(pool)
                add_load(a)
                mod_store(a, a % 2)

            def broadcast_rows(dst, first, semaphore):
                src = mod[bass.ds(first, 2)].rearrange("a n -> (a n)").unsqueeze(0).broadcast_to([P, D])
                pool.dma_start(dst[:], src).then_inc(semaphore, 16)

            def expert(l, e, odd, last):
                E = l * NE + e
                if not last:
                    pool.wait_ge(xgT_ready, E * 2 + 2)
                    apart(pool)
                    pool.tensor_copy(idx_next[:, 1 - odd:2 - odd], idx[:, bass.ds(e + 1, 1)])
                    pool.drain()
                    pool.indirect_dma_start(xg[:, 1 - odd], None, h_rows,
                                            bass.IndirectOffsetOnAxis(ap=idx_next[:, 1 - odd:2 - odd], axis=0)
                                            ).then_inc(gathered[1 - odd], 16)
                pool.wait_ge(y_copied, E + 2)
                apart(pool)
                pool.dma_start(y_rows[bass.ds(e * CAP, CAP)], y_out[0:CAP, odd]).then_inc(row_stored[odd], 16)

            apart(pool)
            with pool.Fori(0, DEPTH) as l:
                pool.wait_ge(x_final, l * NT + NT)
                for p in range(2):
                    pool.wait_ge(mod_stored[p], l * 96 + 32)
                apart(pool)
                broadcast_rows(shift_row, l * NADA, norm_rows)
                broadcast_rows(scale_row, l * NADA + 2, norm_rows)
                pool.dma_start(x_state, x[:].rearrange("p t d -> p (t d)")).then_inc(x_saved, 16)
                pool.dma_start(pw[:].rearrange("p g d -> p (g d)"), pool_w[bass.ds(l, 1)].rearrange("o p n -> (o p) n")).then_inc(pw_landed, 16)
                pool.dma_start(pscale[:], pool_scale[bass.ds(l, 1)].rearrange("o p n -> (o p) n")).then_inc(pw_landed, 16)
                pool.wait_ge(h_ready, l * 8 + 4)
                pool.wait_ge(x_saved, l * 16 + 16)
                apart(pool)
                pool.dma_start(rope[:].rearrange("p a t d -> p (a t d)"), rotary).then_inc(rope_landed, 16)
                for n in range(0, NOV * CAP, T):
                    rows = min(T, NOV * CAP - n)
                    first = NE * CAP + n
                    pool.dma_start(y_rows[first:first + rows], x_state.rearrange("p (t d) -> (p t) d", d=D)[0:rows]
                                   ).then_inc(y_filled, 16)
                for a in range(NADA):
                    a_all = l * NADA + (4 + a)
                    pool.wait_ge(ada_row_ready, a_all)
                    apart(pool)
                    add_load(a_all)
                    mod_store(a_all, a % 2)
                    if a == 1:
                        for p in range(2):
                            pool.wait_ge(mod_stored[p], l * 96 + 48)
                        apart(pool)
                        broadcast_rows(gate_row, l * NADA + 4, gate_landed)
                    if a == 5:
                        for p in range(2):
                            pool.wait_ge(mod_stored[p], l * 96 + 80)
                        apart(pool)
                        broadcast_rows(shift_row, l * NADA + 6, norm_rows)
                        broadcast_rows(scale_row, l * NADA + 8, norm_rows)
                pool.wait_ge(unit_ready, l * NUNIT + (UNIT0["m1"] + 4))
                apart(pool)
                pool.dma_start(x[:].rearrange("p t d -> p (t d)"), x_state).then_inc(x_back, 16)
                pool.wait_ge(x_added, l * 8 + 8)
                for p in range(2):
                    pool.wait_ge(mod_stored[p], l * 96 + 96)
                apart(pool)
                broadcast_rows(gate_row, l * NADA + 10, gate_landed)
                for t in range(NT):
                    pool.wait_ge(h_ready, l * 8 + (4 + t + 1))
                    apart(pool)
                    pool.dma_start(h_rows[t * P:(t + 1) * P], h_nat[:, t % 2]).then_inc(row_stored[t % 2], 16)
                for p in range(2):
                    pool.wait_ge(row_stored[p], l * 160 + 32)
                pool.wait_ge(idx_ready, l + 1)
                apart(pool)
                pool.indirect_dma_start(xg[:, 0], None, h_rows, bass.IndirectOffsetOnAxis(ap=idx[:, 0:1], axis=0)
                                        ).then_inc(gathered[0], 16)
                apart(pool)
                with pool.Fori(0, NE // 2 - 1) as j:
                    expert(l, j * 2, 0, False)
                    expert(l, j * 2 + 1, 1, False)
                expert(l, NE - 2, 0, False)
                expert(l, NE - 1, 1, True)
                for p in range(2):
                    pool.wait_ge(row_stored[p], l * 160 + 160)
                pool.wait_ge(y_filled, l * FILLS + FILLS)
                apart(pool)

                before, count = overflow_blocks(pool, l)
                with pool.If(count > 0):
                    apart(pool)
                    with pool.Fori(0, count) as slot:
                        b = slot + before
                        e = pool.value_load(ov_expert[0:1, bass.ds(slot, 1)], min_val=0, max_val=NE - 1)
                        pool.wait_ge(ov_step, b * OV_STEPS + 3)
                        apart(pool)
                        pool.indirect_dma_start(o_x[:], None, h_rows, bass.IndirectOffsetOnAxis(ap=o_idx[:, 0:1], axis=0)
                                                ).then_inc(ov_x, 16)
                        for n in range(EXP):
                            pool.wait_ge(ov_step, b * OV_STEPS + (5 + n if n < 8 else 17 + n - 8))
                            apart(pool)
                            pool.dma_start(o_w[:], w[bass.ds(l * RAW + e * EXP + (PRE + RAW_MIX + n), 1)].rearrange("o p n -> (o p) n")
                                           ).then_inc(ov_w, 16)
                        pool.wait_ge(ov_step, b * OV_STEPS + OV_STEPS)
                        apart(pool)
                        pool.dma_start(y_rows[bass.ds(slot * CAP + NE * CAP, CAP)], o_y[0:CAP]).then_inc(ov_y, 16)
                        pool.wait_ge(ov_y, b * 16 + 16)
                apart(pool)
                pool.nop()

                for t in range(NT):
                    if t >= 2:
                        pool.wait_ge(x_final, l * NT + (NT + t - 1))
                    apart(pool)
                    for j in range(2):
                        pool.indirect_dma_start(y_pair[:, t % 2, j], None, y_rows,
                                                bass.IndirectOffsetOnAxis(ap=slot_i[:, 4 * j + t:4 * j + t + 1], axis=0)
                                                ).then_inc(pair_in[t % 2][j], 16)

            pool.dma_start(scale_row[:], final_g.broadcast_to([P, D])).then_inc(norm_rows, 16)
            for t in range(NT):
                pool.wait_ge(norm_done, t + 1)
                apart(pool)
                pool.dma_start(out[t * P:(t + 1) * P], x[:, t]).then_inc(out_stored, 16)
            pool.wait_ge(out_stored, 16 * NT)
            for p in range(2):
                pool.wait_ge(mod_stored[p], 8 * (4 + DEPTH * NADA))


def weight_stream(w_ada, w_in, w_ret_o, w_pool_o, w_out, w_gate, w_up, w_down):
    out = np.empty((PIECES, P, 1024), np.float32)

    def rows(m, j, c):
        return m[256 * j:256 * j + 256, 512 * c:512 * c + 512].reshape(2, P, 512).transpose(1, 0, 2).reshape(P, 1024)

    n = 0
    for c in range(4):
        for j in range(ADA_PIECES):
            out[n] = rows(w_ada[0], j, c)
            n += 1
    group_of = [g for g, m in GROUPS for _ in range(m)]
    for l in range(DEPTH):
        for s in STREAM:
            if s[0] == "ada":
                a, j = s[1:]
                layer, c = (l, 4 + a) if a < 8 else (min(l + 1, DEPTH - 1), a - 8)
                out[n] = rows(w_ada[layer], j, c)
            else:
                g = group_of[s[1]]
                j = s[1] - FIRST[g]
                m, c = {"P": (w_pool_o, int(g[-1] == "1")), "R": (w_ret_o, int(g[-1] == "1")),
                        "O": (w_out, int(g[-1] == "1"))}.get(g[0], (w_in, W_IN_COLUMN.get(g)))
                out[n] = rows(m[l], j, c)
            n += 1
        for e in range(NE):
            for half in range(2):
                cols = slice(256 * half, 256 * half + 256)
                for j in range(4):
                    r = slice(256 * j, 256 * j + 256)
                    both = np.stack([w_gate[l, e, r, cols], w_up[l, e, r, cols]], 1)
                    out[n] = both.reshape(2, P, 512).transpose(1, 0, 2).reshape(P, 1024)
                    n += 1
            out[n:n + 4] = w_down[l, e].reshape(4, P, 1024)
            n += 4
    assert n == PIECES
    return out


def kernel(x, c, w_ada, b_ada, norm1_g, norm2_g, w_in, w_ret_o, pool_w, pool_scale, w_pool_o, w_out,
           w_router, b_router, w_e_gate, w_e_up, w_e_down, final_g):
    import concourse.bacc as bacc
    from concourse.bass_utils import run_bass_kernel_spmd

    f = [np.asarray(a) for a in (x, c, w_ada, b_ada, norm1_g, norm2_g, w_in, w_ret_o, pool_w, pool_scale, w_pool_o,
                                 w_out, w_router, b_router, w_e_gate, w_e_up, w_e_down, final_g)]
    (x, c, w_ada, b_ada, norm1_g, norm2_g, w_in, w_ret_o, pool_w, pool_scale, w_pool_o, w_out, w_router, b_router,
     w_e_gate, w_e_up, w_e_down, final_g) = f

    consts = constants()
    o, n = CONST_AT["wr"]
    consts[:, o:o + n] = w_router.reshape(8, P, NE).transpose(1, 0, 2).reshape(P, n)
    o, n = CONST_AT["br"]
    consts[:, o:o + n] = b_router[None, :]
    ada_rows = np.zeros((4 + DEPTH * NADA, 2, 512), np.float32)
    for a in range(4 + DEPTH * NADA):
        l, col = divmod(a, NADA)
        if l == DEPTH:
            l = DEPTH - 1
        ada_rows[a, 0] = b_ada[l, 512 * col:512 * col + 512]
        if col in (2, 3):
            ada_rows[a, 1] = norm1_g[l, 512 * (col - 2):512 * (col - 1)]
        if col in (8, 9):
            ada_rows[a, 1] = norm2_g[l, 512 * (col - 8):512 * (col - 7)]
    arrays = {
        "w": weight_stream(w_ada, w_in, w_ret_o, w_pool_o, w_out, w_e_gate, w_e_up, w_e_down),
        "x_in": np.ascontiguousarray(x.reshape(NT, P, D).transpose(1, 0, 2).reshape(P, NT * D)),
        "c_in": np.ascontiguousarray(c.reshape(8, P).T),
        "consts": consts,
        "rotary": rotary_tables().reshape(P, 2 * NT * DK),
        "ada_rows": ada_rows.reshape(-1, 1024),
        "pool_w": np.ascontiguousarray(pool_w.transpose(0, 2, 1, 3).reshape(DEPTH, P, 512)),
        "pool_scale": np.ascontiguousarray(pool_scale.reshape(DEPTH, 4, P).transpose(0, 2, 1)),
        "final_g": np.ascontiguousarray(final_g.reshape(1, D)),
    }
    nc = bacc.Bacc("TRN2", target_bir_lowering=False, num_devices=1)
    args = [nc.dram_tensor(name, a.shape, mybir.dt.from_np(a.dtype), kind="ExternalInput").ap()
            for name, a in arrays.items()]
    out = nc.dram_tensor("out", (T, D), F32, kind="ExternalOutput").ap()
    build(nc, *args, out)
    r = run_bass_kernel_spmd(nc, [arrays], core_ids=[0])
    return r.results[0]["out"].reshape(1, T, D)
```

```python
from contextlib import ExitStack

import numpy as np

import concourse.bass as bass
from concourse import mybir

F32 = mybir.dt.float32
F32R = mybir.dt.float32r
I32 = mybir.dt.int32
ALU = mybir.AluOpType
ACT = mybir.ActivationFunctionType
AX = mybir.AxisListType.X

P = 128
D = 1024
T = 512
DEPTH = 2
NT = T // P
HEADS = 4
DK = 128
DV = 256
WINDOWS = (2, 4, 8, 16)
NE = 16
NG = 4
EPS = 1e-6
CAP = 128
LEVELS = T // CAP
NOV = 2 * T // CAP - 1
NSLOT = (NE + NOV) * CAP

GROUPS = [("q", 4), ("k", 4), ("v0", 4), ("v1", 4), ("u", 4), ("g0", 4), ("g1", 4), ("ap0", 4), ("P0", 2),
          ("ap1", 4), ("P1", 2), ("ar0", 4), ("R0", 4), ("ar1", 4), ("R1", 4), ("O0", 4), ("O1", 4)]
NAMES = [g for g, _ in GROUPS]
W_IN_COLUMN = {"q": 0, "k": 1, "v0": 2, "v1": 3, "g0": 4, "g1": 5, "u": 6, "ar0": 7, "ar1": 8, "ap0": 9, "ap1": 10}
FIRST = {g: sum(n for _, n in GROUPS[:i]) for i, (g, _) in enumerate(GROUPS)}
LAST = {g: FIRST[g] + n - 1 for g, n in GROUPS}
NGROUP = len(GROUPS)
MIX = sum(n for _, n in GROUPS)
EXP = 12
PROD = MIX + EXP * NE
NADA = 12
ADA_PIECES = 4
RAW_SLOTS = 8
W_SLOTS = 4
PRE = 4 * ADA_PIECES
RAW_MIX = MIX + NADA * ADA_PIECES
RAW = RAW_MIX + EXP * NE
PIECES = PRE + DEPTH * RAW
AHEAD = 8
LANDS = 16 * (RAW - AHEAD) // RAW_SLOTS


def layer_stream():
    out = [("w", q) for q in range(W_SLOTS)]
    for q in range(MIX):
        ends = [i for i, g in enumerate(NAMES) if LAST[g] == q]
        if ends and ends[0] < NADA:
            out += [("ada", ends[0], j) for j in range(ADA_PIECES)]
        if q + W_SLOTS < MIX:
            out.append(("w", q + W_SLOTS))
    return out


STREAM = layer_stream()
RAW_OF_W = {s[1]: r for r, s in enumerate(STREAM) if s[0] == "w"}
RAW_OF_ADA = {s[1:]: r for r, s in enumerate(STREAM) if s[0] == "ada"}

UNIT_LIST = [("h1", 8), ("q", 4), ("k", 4), ("mix", 4), ("y", 8), ("pw", 4), ("m0", 4), ("m1", 4), ("h2", 8)]
UNITS = dict(UNIT_LIST)
UNIT0 = {name: sum(n for _, n in UNIT_LIST[:i]) for i, (name, _) in enumerate(UNIT_LIST)}
NUNIT = sum(UNITS.values())
SPLIT_LIST = [u for u in UNIT_LIST if u[0] not in ("q", "k", "mix")]
SPLIT0 = {name: sum(n for _, n in SPLIT_LIST[:i]) for i, (name, _) in enumerate(SPLIT_LIST)}
NSPLIT = sum(n for _, n in SPLIT_LIST)

CONST_WIDTH = [("ident", P), ("causal", P), ("before", P), ("ones", P), ("iota", P), ("diag", 4 * P),
               ("diag0", 64), ("off", 64), ("xi", 4), ("vscale", 4), ("tokid", 4), ("rev16", 16), ("rev4", 4),
               ("ecap", 16), ("blockid", NOV), ("eid", 16), ("eps", 1), ("wr", 8 * NE), ("br", NE)]
CONST_AT = {}
NCONST = 0
for _name, _n in CONST_WIDTH:
    CONST_AT[_name] = (NCONST, _n)
    NCONST += _n
GAMMA = [1.0 - 2.0 ** (-5.0 - h) for h in range(HEADS)]
GAMMA_C = [g ** P for g in GAMMA]


def constants():
    c = np.zeros((P, NCONST), np.float32)

    def put(name, a):
        o, n = CONST_AT[name]
        c[:, o:o + n] = np.asarray(a, np.float64).reshape(P, n)

    i = np.arange(P)
    put("ident", np.eye(P))
    put("causal", (i[None, :] >= i[:, None]))
    put("before", (i[:, None] < i[None, :]))
    put("ones", np.ones((P, P)))
    put("iota", np.tile(i, (P, 1)))
    diag, diag0, off = np.zeros((P, 4, P)), np.zeros((P, 4, 16)), np.zeros((P, 4, 16))
    for g, w in enumerate(WINDOWS):
        a = np.zeros((2 * P, 2 * P))
        for s in range(2 * P):
            lo = max(s + 1 - w, 0)
            a[s, lo:s + 1] = np.float32(1.0) / np.float32(s + 1 - lo)
            a[s, s] -= 1.0
        diag[:, g], diag0[:, g], off[:, g] = a[P:, P:].T, a[:16, :P].T, a[P:P + 16, :P].T
    put("diag", diag)
    put("diag0", diag0)
    put("off", off)
    g = np.array(GAMMA)
    put("xi", g[None, :] ** (i[:, None] + 1.0))
    put("vscale", g[None, :] ** -(i[:, None] + 1.0) * DK ** -0.5)
    put("tokid", i[:, None] + P * np.arange(NT)[None, :])
    put("rev16", np.tile(16 - np.arange(16), (P, 1)))
    put("rev4", np.tile(4 - np.arange(4), (P, 1)))
    put("ecap", np.tile(CAP * np.arange(16), (P, 1)))
    put("blockid", np.tile(np.arange(NOV), (P, 1)))
    put("eid", np.tile(np.arange(16), (P, 1)))
    put("eps", np.full((P, 1), EPS))
    return c


def rotary_tables():
    freqs = np.float32(10000.0) ** (-np.arange(0, DK, 2, dtype=np.float32) / np.float32(DK))
    ang = (np.arange(T, dtype=np.float32)[:, None] * freqs[None, :]).astype(np.float32).astype(np.float64)
    cos, sin = np.cos(ang), np.sin(ang)
    both = np.stack([np.concatenate([cos, cos], 1), np.concatenate([-sin, sin], 1)])
    return np.ascontiguousarray(both.reshape(2, NT, P, DK).transpose(2, 0, 1, 3).astype(np.float32))


def build(nc, w, x_in, c_in, consts, rotary, ada_rows, pool_w, pool_scale, final_g, out):
    mod = nc.dram_tensor("mod_rows", (4 + DEPTH * NADA, 512), F32, kind="Internal").ap()
    x_state = nc.dram_tensor("x_state", (P, NT * D), F32, kind="Internal").ap()
    h_rows = nc.dram_tensor("h_rows", (T, D), F32, kind="Internal").ap()
    y_rows = nc.dram_tensor("y_rows", (NSLOT, D), F32, kind="Internal").ap()

    with ExitStack() as ctx:
        def sem(name):
            return ctx.enter_context(nc.semaphore(name))

        at = (nc.sbuf_base + 63) // 64 * 64

        def region(kib):
            nonlocal at
            at += int(kib * 1024)
            return at - int(kib * 1024)

        def sb(name, shape, dtype, offset):
            return nc.alloc_sbuf_tensor_at(name, shape, dtype, offset=offset)

        raw = sb("raw", [P, RAW_SLOTS, 1024], F32, region(32))
        w_hi = sb("w_hi", [P, W_SLOTS, 1024], F32R, region(16))
        w_lo = sb("w_lo", [P, W_SLOTS, 1024], F32R, region(16))
        hT_hi = sb("hT_hi", [P, 8, T], F32R, region(16))
        hT_lo = sb("hT_lo", [P, 8, T], F32R, region(16))
        ahead = sb("ahead", [P, AHEAD, 1024], F32, at - 32 * 1024)

        A = region(32)
        q_rot = sb("q_rot", [P, NT, 512], F32, A)
        k_rot = sb("k_rot", [P, NT, 512], F32, A + 8192)
        qT = sb("qT", [P, HEADS, T], F32, A + 16384)
        kT = sb("kT", [P, HEADS, T], F32, A + 24576)
        yT_hi = sb("yT_hi", [P, 8, T], F32R, A)
        yT_lo = sb("yT_lo", [P, 8, T], F32R, A + 16384)
        xg = sb("xg", [P, 2, D], F32, A)
        xgT_hi = sb("xgT_hi", [P, 2, D], F32R, A + 8192)
        xgT_lo = sb("xgT_lo", [P, 2, D], F32R, A + 16384)
        hid = sb("hid", [P, 512], F32, A + 24576)
        hidT_hi = sb("hidT_hi", [P, 512], F32R, A + 26624)
        hidT_lo = sb("hidT_lo", [P, 512], F32R, A + 28672)
        y_pair = sb("y_pair", [P, NT, 2, D], F32, A)
        o_hot = sb("o_hot", [P, 8, P], F32, A)
        o_x = sb("o_x", [P, D], F32, A + 4096)
        o_xT = sb("o_xT", [P, 8, P], F32, A + 8192)
        o_w = sb("o_w", [P, 1024], F32, A + 12288)
        o_sig = sb("o_sig", [P, 2, 256], F32, A + 16384)
        o_hid = sb("o_hid", [P, 512], F32, A + 18432)
        o_hidT = sb("o_hidT", [P, 4, P], F32, A + 20480)
        hot = sb("hot", [P, 2, NT, P], F32R, A + 24576)

        B = region(16)
        y = sb("y", [P, NT, D], F32, B)
        ypT_hi = sb("ypT_hi", [P, 4, T], F32R, B)
        ypT_lo = sb("ypT_lo", [P, 4, T], F32R, B + 8192)
        y_out = sb("y_out", [P, 2, D], F32, B)
        squares = sb("squares", [P, D], F32, B)
        o_y = sb("o_y", [P, D], F32, B + 8192)

        C = region(16)
        x = sb("x", [P, NT, D], F32, C)
        rope = sb("rope", [P, 2, NT, DK], F32, C)
        u = sb("u", [P, NT, 512], F32, C)
        mixT = sb("mixT", [P, 4, T], F32, C + 8192)
        merged = sb("merged", [P, 2, NT, 512], F32, C)

        Dr = region(11)
        scores = sb("scores", [P, 2, T], F32, Dr)
        kv_sum = sb("kv_sum", [P, 3, DV], F32, Dr + 4096)
        state = sb("state", [P, 3, DV], F32, Dr + 7168)
        y_sq = sb("y_sq", [P, DV], F32, Dr + 10240)
        h_nat = sb("h_nat", [P, 2, D], F32, Dr)
        sig_ret = sb("sig_ret", [P, NT, 512], F32, Dr)

        shift_row = sb("shift_row", [P, D], F32, region(4))
        scale_row = sb("scale_row", [P, D], F32, region(4))
        gate_row = sb("gate_row", [P, D], F32, region(4))
        ada_acc = sb("ada_acc", [P, 2, 512], F32, region(4))
        ada_add = sb("ada_add", [1, 2, 512], F32, region(4))
        ada_row = sb("ada_row", [1, 512], F32, region(2))
        tmp = sb("tmp", [P, 2, 512], F32, region(4))
        const_at = region(-(-NCONST * 4 // 64) / 16)
        const = sb("const", [P, NCONST], F32, const_at)
        before_r = sb("before_r", [P, P], F32R, const_at + 4 * CONST_AT["before"][0])
        pw = sb("pw", [P, 4, P], F32, region(2))

        def small(name, n, dtype=F32):
            return sb(name, [P, n], dtype, region(((n * 4 + 63) // 64) * 64 / 1024))

        router_at = B + 8192

        def router_small(name, n, dtype=F32):
            nonlocal router_at
            router_at += (n * 4 + 63) // 64 * 64
            return sb(name, [P, n], dtype, router_at - (n * 4 + 63) // 64 * 64)

        pscale = small("pscale", 4)
        cond = small("cond", 8)
        cond_raw = small("cond_raw", 8)
        wr_hi = small("wr_hi", 8 * NE, F32R)
        wr_lo = small("wr_lo", 8 * NE, F32R)
        ones_r = small("ones_r", P, F32R)
        y_ss = small("y_ss", 16)
        y_std = small("y_std", 16)
        y_rs = small("y_rs", 16)
        x_ss = small("x_ss", 4)
        x_std = small("x_std", 4)
        x_rs = small("x_rs", 4)
        lgT = router_small("lgT", T)
        lg = router_small("lg", 64)
        probs = router_small("probs", 64)
        s4 = router_small("s4", 16)
        s4b = router_small("s4b", 16)
        rt = router_small("rt", 64)
        pairs = router_small("pairs", 96)
        r1 = router_small("r1", 4)
        top = router_small("top", 8)
        wts = small("wts", 8)
        hot1 = router_small("hot1", 64)
        hot2 = router_small("hot2", 64)
        chosen = router_small("chosen", 64, F32R)
        pos = router_small("pos", 64)
        ovn = router_small("ovn", 16)
        ovc = router_small("ovc", 32)
        ovd = router_small("ovd", 32)
        slotf = small("slotf", 8)
        posk = router_small("posk", 8)
        hotid = router_small("hotid", 128, F32R)
        ovt = router_small("ovt", 16 * NOV)
        ovt2 = router_small("ovt2", 16 * NOV)
        ov_range_f = small("ov_range_f", 2)
        ov_base = small("ov_base", 1)
        slot_i = small("slot_i", 8, I32)
        idx = small("idx", 16, I32)
        ov_range = small("ov_range", 2, I32)
        ov_expert = small("ov_expert", NOV, I32)
        o_idx = small("o_idx", 1, I32)
        idx_next = small("idx_next", 2, I32)
        assert at <= 229344 and router_at <= B + 16384

        def k(name):
            o, n = CONST_AT[name]
            return const[:, o:o + n]

        ps = ctx.enter_context(nc.psum_tensor("ps", [P, 8, 512], F32))
        ident = k("ident")

        landed = [sem(f"raw_landed{s}") for s in range(RAW_SLOTS)]
        ahead_landed = [sem(f"ahead_landed{i}") for i in range(2)]
        raw_used = sem("raw_used")
        w_hi_ready = sem("w_hi_ready")
        w_used = sem("w_used")
        acc_ready = sem("acc_ready")
        acc_free = sem("acc_free")
        unit_ready = sem("unit_ready")
        unit_hi = sem("unit_hi")
        unit_free = sem("unit_free")
        x_landed = sem("x_landed")
        c_landed = sem("c_landed")
        consts_landed = sem("consts_landed")
        cond_sig = sem("cond_sig")
        wr_hi_ready = sem("wr_hi_ready")
        x_std_ready = sem("x_std_ready")
        h_ready = sem("h_ready")
        rot_done = sem("rot_done")
        score_ready = sem("score_ready")
        score_masked = sem("score_masked")
        kv_ready = sem("kv_ready")
        kv_used = sem("kv_used")
        state_ready = sem("state_ready")
        y_ready = sem("y_ready")
        y_read = sem("y_read")
        y_std_ready = sem("y_std_ready")
        gate_sig = sem("gate_sig")
        gated = sem("gated")
        merged_add = sem("merged_add")
        x_added = sem("x_added")
        x_final = sem("x_final")
        ada_mac = sem("ada_mac")
        ada_sum = sem("ada_sum")
        ada_row_ready = sem("ada_row_ready")
        ada_add_landed = sem("ada_add_landed")
        mod_stored = [sem(f"mod_stored{i}") for i in range(2)]
        x_saved = sem("x_saved")
        x_back = sem("x_back")
        rope_landed = sem("rope_landed")
        pw_landed = sem("pw_landed")
        norm_rows = sem("norm_rows")
        gate_landed = sem("gate_landed")
        row_stored = [sem(f"row_stored{i}") for i in range(2)]
        logitsT_ready = sem("logitsT_ready")
        logitsT_copied = sem("logitsT_copied")
        logits_ready = sem("logits_ready")
        max_off = sem("max_off")
        exp_done = sem("exp_done")
        chosen_ready = sem("chosen_ready")
        pos_ready = sem("pos_ready")
        hot_ready = sem("hot_ready")
        idx_sum = sem("idx_sum")
        idx_ready = sem("idx_ready")
        gathered = [sem(f"gathered{i}") for i in range(2)]
        xgT_ready = sem("xgT_ready")
        xgT_hi_ready = sem("xgT_hi_ready")
        xgT_lo_ready = sem("xgT_lo_ready")
        act_sig = sem("act_sig")
        hid_ready = sem("hid_ready")
        hidT_ready = sem("hidT_ready")
        hidT_hi_ready = sem("hidT_hi_ready")
        hidT_lo_ready = sem("hidT_lo_ready")
        y_copied = sem("y_copied")
        slots_ready = sem("slots_ready")
        pair_in = [sem(f"pair_in{i}") for i in range(NT)]
        ov_step = sem("ov_step")
        ov_w = sem("ov_w")
        ov_x = sem("ov_x")
        ov_y = sem("ov_y")
        norm_done = sem("norm_done")
        y_filled = sem("y_filled")
        out_stored = sem("out_stored")
        steps = sem("steps")

        block = ctx.enter_context(nc.Block())

        def land_value(l, r):
            return l * LANDS + 16 * ((PRE + r) // RAW_SLOTS + 1)

        def raw_value(l, r):
            return l * RAW + (PRE + r + 1 + RAW_SLOTS)

        def w_done(l, q):
            return l * PROD + (q + 1 + W_SLOTS)

        def acc_value(l, g, t):
            return l * (4 * NGROUP) + (4 * g + t + 1 + 4)

        def unit_value(l, name, n):
            return l * NUNIT + (UNIT0[name] + n + 1)

        OV_STEPS = 22
        FILLS = 16 * -(-NOV * CAP // T)

        def apart(eng):
            eng.sem_inc(steps, 1)

        @block.sync
        def _(sp):
            def load(piece, s, used):
                sp.wait_ge(raw_used, used)
                sp.dma_start(raw[:, s], w[bass.ds(piece, 1)].rearrange("o p n -> (o p) n")).then_inc(landed[s], 16)

            for piece in range(PRE):
                load(piece, piece % RAW_SLOTS, piece + 1)
            with sp.Fori(0, DEPTH) as l:
                with sp.Fori(0, (RAW_MIX + AHEAD) // RAW_SLOTS) as i:
                    for s in range(RAW_SLOTS):
                        load(l * RAW + i * RAW_SLOTS + (PRE + s), s, l * RAW + i * RAW_SLOTS + (PRE + s + 1))
                sp.wait_ge(logitsT_ready, l + 1)
                for i in range(2):
                    first = PRE + RAW_MIX + RAW_SLOTS + 4 * i
                    sp.dma_start(ahead[:, 4 * i:4 * i + 4], w[bass.ds(l * RAW + first, 4)].rearrange("o p n -> p o n")
                                 ).then_inc(ahead_landed[i], 16)
                for s in range(RAW_SLOTS):
                    first = PRE + RAW_MIX + RAW_SLOTS + AHEAD + s
                    load(l * RAW + first, s, l * RAW + (first + 1 - AHEAD))
                with sp.Fori((RAW_MIX + AHEAD) // RAW_SLOTS + 2, RAW // RAW_SLOTS) as i:
                    for s in range(RAW_SLOTS):
                        load(l * RAW + i * RAW_SLOTS + (PRE + s), s, l * RAW + i * RAW_SLOTS + (PRE + s + 1))

        def overflow_blocks(eng, l):
            apart(eng)
            start = eng.value_load(ov_range[0:1, 0:1], min_val=0, max_val=DEPTH * NOV)
            count = eng.value_load(ov_range[0:1, 1:2], min_val=0, max_val=NOV)
            return start, count

        def expert_piece(first, n, r):
            return ahead[:, n - RAW_SLOTS] if first and n >= RAW_SLOTS else raw[:, r % RAW_SLOTS]

        @block.scalar
        def _(act):
            act.sem_inc(state_ready, 3)
            act.wait_ge(consts_landed, 16)
            act.activation(before_r[:], k("before"), ACT.Copy)
            act.activation(ones_r[:], k("ones"), ACT.Copy)
            act.activation(wr_hi[:], k("wr"), ACT.Copy).then_inc(wr_hi_ready, 1)
            act.wait_ge(c_landed, 16)
            act.activation(cond[:], cond_raw[:], ACT.Sigmoid).then_inc(cond_sig, 1)

            def hi(l, q, r):
                act.wait_ge(landed[r % RAW_SLOTS], land_value(l, r))
                act.wait_ge(w_used, l * PROD + (q + 1))
                act.activation(w_hi[:, q % W_SLOTS], raw[:, r % RAW_SLOTS], ACT.Copy).then_inc(w_hi_ready, 1)

            def row_deviations(t):
                act.activation(squares[:], x[:, t], ACT.Square, accum_out=x_ss[:, t:t + 1])
                act.drain()
                act.activation(x_std[:, t:t + 1], x_ss[:, t:t + 1], ACT.Sqrt, bias=k("eps"),
                               scale=1.0 / D).then_inc(x_std_ready, 1)

            def unit_hi_half(l, name, n, dst, scale=1.0):
                act.wait_ge(unit_ready, unit_value(l, name, n))
                bank = 4 + (UNIT0[name] + n) % 2
                act.activation(dst, ps[:, bank].rearrange("p (a b) -> p a b", a=4) if len(dst.shape) == 3 else ps[:, bank],
                               ACT.Copy, scale=scale).then_inc(unit_hi, 1)

            def transposed_hi(l, name, dst, tiles, quads):
                n = 0
                for t in tiles:
                    for j in quads:
                        unit_hi_half(l, name, n, dst[:, 4 * j:4 * j + 4, t * P:(t + 1) * P])
                        n += 1

            def norm_hi(l, name, t):
                for j in range(2):
                    unit_hi_half(l, name, 2 * t + j, hT_hi[:, 4 * j:4 * j + 4, t * P:(t + 1) * P])

            def retention_head(l, h):
                for n in range(3):
                    i = 3 * h + n
                    act.wait_ge(kv_used, l * 12 + (i + 1 + 2))
                    act.activation(state[:, n], kv_sum[:, n], ACT.Copy, scale=GAMMA_C[h]).then_inc(state_ready, 1)
                for n in range(NT):
                    act.wait_ge(y_read, l * 16 + (4 * h + n + 1 + 2))
                    act.activation(y_sq[:], y[:, n, h * DV:(h + 1) * DV], ACT.Square,
                                   accum_out=y_ss[:, 4 * h + n:4 * h + n + 1])
                    act.drain()

            def retention_pair(l, h0):
                retention_head(l, h0)
                retention_head(l, h0 + 1)

            def head_deviations(l, pair):
                act.activation(y_std[:, 8 * pair:8 * pair + 8], y_ss[:, 8 * pair:8 * pair + 8], ACT.Sqrt,
                               bias=k("eps"), scale=1.0 / DV).then_inc(y_std_ready, 1)

            def acc_wait(l, g, t):
                if t < 3:
                    act.wait_ge(acc_ready, l * (3 * NGROUP) + (3 * g + t + 1))
                else:
                    act.wait_ge(w_used, w_done(l, LAST[NAMES[g]]))

            def read_group(l, g):
                name = NAMES[g]
                for t in range(NT):
                    if name in ("v0", "v1"):
                        half = int(name[1])
                        acc_wait(l, g, t)
                        for j in range(2):
                            h = 2 * half + j
                            last = act.activation(y[:, t, h * DV:(h + 1) * DV], ps[:, t, j * DV:(j + 1) * DV],
                                                  ACT.Copy, scale=k("vscale")[:, h:h + 1])
                        last.then_inc(acc_free, 1)
                    elif name == "u":
                        if t == 0:
                            act.wait_ge(x_saved, l * 16 + 16)
                        acc_wait(l, g, t)
                        act.activation(u[:, t], ps[:, t], ACT.Copy).then_inc(acc_free, 1)
                    elif name in ("g0", "g1"):
                        acc_wait(l, g, t)
                        act.wait_ge(gated, l * 8 + (4 * int(name[1]) + t + 1))
                        act.activation(tmp[:, t % 2], ps[:, t], ACT.Sigmoid).then_inc(gate_sig, 1)
                    elif name in ("ap0", "ap1"):
                        acc_wait(l, g, t)
                        act.activation(merged[:, int(name[2]), t], ps[:, t], ACT.Sigmoid).then_inc(acc_free, 1)
                    elif name in ("ar0", "ar1"):
                        acc_wait(l, g, t)
                        if name == "ar1":
                            act.wait_ge(merged_add, l * 8 + (t + 1))
                        act.activation(sig_ret[:, t], ps[:, t], ACT.Sigmoid).then_inc(acc_free, 1)

            def misc(l, name):
                if name == "u":
                    retention_pair(l, 0)
                    retention_pair(l, 2)
                    head_deviations(l, 0)
                    head_deviations(l, 1)
                elif name == "ap0":
                    transposed_hi(l, "y", yT_hi, range(NT), range(2))
                    for g in range(4):
                        unit_hi_half(l, "pw", g, ypT_hi[:, g], scale=pscale[:, g:g + 1])
                elif name == "ar1":
                    transposed_hi(l, "m0", hT_hi, range(NT), [0])
                elif name == "R1":
                    transposed_hi(l, "m1", hT_hi, range(NT), [1])

            def expert(l, e, odd, first=False, last=False):
                E = l * NE + e
                q0 = l * PROD + e * EXP

                def hi_e(n):
                    r = 12 * odd + n
                    if first and n >= RAW_SLOTS:
                        act.wait_ge(ahead_landed[(n - RAW_SLOTS) // 4], l * 16 + 16)
                    else:
                        base = l * LANDS + (e - odd) * (16 * EXP // RAW_SLOTS)
                        turn = (PRE + RAW_MIX + r) // RAW_SLOTS + (1 if first else 0)
                        act.wait_ge(landed[r % RAW_SLOTS], base + 16 * turn)
                    act.wait_ge(w_used, q0 + (MIX + n + 1))
                    act.activation(w_hi[:, n % W_SLOTS], expert_piece(first, n, r), ACT.Copy).then_inc(w_hi_ready, 1)

                def sig(half):
                    act.wait_ge(w_used, q0 + (MIX + 4 * half + 4 + W_SLOTS))
                    act.activation(tmp[:, half, 0:256], ps[:, half, 0:256], ACT.Sigmoid).then_inc(act_sig, 1)

                def hidT(half):
                    act.wait_ge(hidT_ready, E * 2 + (half + 1))
                    act.activation(hidT_hi[:, 256 * half:256 * half + 256], ps[:, 6 + half, 0:256],
                                   ACT.Copy).then_inc(hidT_hi_ready, 1)

                hi_e(4)
                hi_e(5)
                sig(0)
                hi_e(6)
                hi_e(7)
                hidT(0)
                hi_e(8)
                hi_e(9)
                sig(1)
                hi_e(10)
                hi_e(11)
                hidT(1)
                if not last:
                    hi_e(12)
                    hi_e(13)
                    gathered_hi(E + 1, 1 - odd)
                    hi_e(14)
                    hi_e(15)

            def gathered_hi(E, slot):
                for j in range(2):
                    act.wait_ge(xgT_ready, E * 2 + (j + 1 + 2))
                    act.activation(xgT_hi[:, slot, 512 * j:512 * j + 512], ps[:, 4 + j], ACT.Copy).then_inc(xgT_hi_ready, 1)

            for q in range(W_SLOTS):
                hi(0, q, RAW_OF_W[q])
            apart(act)
            with act.Fori(0, DEPTH) as l:
                for t in range(NT):
                    act.wait_ge(x_final, l * NT + (t + 1))
                    row_deviations(t)
                for t in range(NT):
                    norm_hi(l, "h1", t)
                for q in range(MIX):
                    for g in range(NGROUP):
                        if LAST[NAMES[g]] == q:
                            read_group(l, g)
                            misc(l, NAMES[g])
                    if q + W_SLOTS < MIX:
                        hi(l, q + W_SLOTS, RAW_OF_W[q + W_SLOTS])
                for t in range(NT):
                    act.wait_ge(x_added, l * 8 + (4 + t + 1))
                    row_deviations(t)
                    if t >= 2:
                        norm_hi(l, "h2", t - 2)
                norm_hi(l, "h2", 2)
                norm_hi(l, "h2", 3)
                act.wait_ge(logitsT_ready, l + 1)
                act.activation(lgT[0:NE], ps[0:NE, 6], ACT.Copy).then_inc(logitsT_copied, 1)
                for q in range(W_SLOTS):
                    hi(l, MIX + q, RAW_MIX + q)
                act.wait_ge(max_off, l + 1)
                act.activation(probs[:], lg[:], ACT.Exp).then_inc(exp_done, 1)
                gathered_hi(l * NE, 0)
                expert(l, 0, 0, first=True)
                expert(l, 1, 1)
                apart(act)
                with act.Fori(1, NE // 2 - 1) as j:
                    expert(l, j * 2, 0)
                    expert(l, j * 2 + 1, 1)
                expert(l, NE - 2, 0)
                expert(l, NE - 1, 1, last=True)

                act.wait_ge(slots_ready, l + 1)
                before, count = overflow_blocks(act, l)
                with act.If(count > 0):
                    apart(act)
                    with act.Fori(0, count) as slot:
                        b = slot + before
                        act.wait_ge(ov_step, b * OV_STEPS + 13)
                        for half in range(2):
                            one = act.activation(o_sig[:, half], ps[:, half, 0:256], ACT.Sigmoid)
                        one.then_inc(ov_step, 1)
                act.nop()
                with act.If(l < DEPTH - 1):
                    for q in range(W_SLOTS):
                        hi(l + 1, q, RAW_OF_W[q])
                act.nop()
            for t in range(NT):
                act.wait_ge(x_final, DEPTH * NT + (t + 1))
                row_deviations(t)

        @block.vector
        def _(v):
            v.sem_inc(raw_used, RAW_SLOTS)
            v.sem_inc(y_copied, 1)
            v.sem_inc(acc_free, 4)
            v.sem_inc(unit_free, 2)
            v.sem_inc(kv_used, 2)
            v.sem_inc(y_read, 2)
            v.sem_inc(gated, 2)
            v.wait_ge(wr_hi_ready, 1)
            v.tensor_tensor(wr_lo[:], k("wr"), wr_hi[:], ALU.subtract)
            v.memset(ov_range_f[:], 0.0)
            v.wait_ge(cond_sig, 1)
            v.drain()
            v.tensor_tensor(cond[:], cond[:], cond_raw[:], ALU.mult)
            v.drain()

            def lo(l, q, r):
                v.wait_ge(w_hi_ready, l * PROD + (q + 1))
                v.tensor_tensor(w_lo[:, q % W_SLOTS], raw[:, r % RAW_SLOTS], w_hi[:, q % W_SLOTS],
                                ALU.subtract).then_inc(raw_used, 1)

            def ada_products(wait_piece, slot0, acc):
                for j in range(ADA_PIECES):
                    wait_piece(j)
                    for i in range(2):
                        piece = raw[:, (slot0 + j) % RAW_SLOTS, 512 * i:512 * i + 512]
                        c = cond[:, 2 * j + i:2 * j + i + 1]
                        if j == 0 and i == 0:
                            one = v.tensor_scalar(ada_acc[:, acc], piece, c, None, ALU.mult)
                        else:
                            one = v.scalar_tensor_tensor(ada_acc[:, acc], piece, c, ada_acc[:, acc], ALU.mult, ALU.add)
                        if i == 1:
                            one.then_inc(raw_used, 1)
                        last = v.drain()
                last.then_inc(ada_mac, 1)

            def ada_finish(a_all, scale):
                v.wait_ge(ada_sum, a_all + 1)
                v.wait_ge(ada_add_landed, (a_all + 1) * 16)
                one = v.tensor_tensor(ada_row[:], ps[0:1, 7], ada_add[:, 0], ALU.add)
                if scale:
                    v.drain()
                    one = v.scalar_tensor_tensor(ada_row[:], ada_row[:], 1.0, ada_add[:, 1], ALU.add, ALU.mult)
                one.then_inc(ada_row_ready, 1)

            def first_products(a):
                ada_products(lambda j: v.wait_ge(landed[(4 * a + j) % RAW_SLOTS], 16 * ((4 * a + j) // RAW_SLOTS + 1)),
                             4 * a, a % 2)

            first_products(0)
            for a in range(4):
                if a < 3:
                    first_products(a + 1)
                if a:
                    v.wait_ge(mod_stored[(a - 1) % 2], 16 * ((a - 1) // 2 + 1))
                ada_finish(a, a >= 2)
            v.wait_ge(x_landed, 16)
            v.sem_inc(x_final, NT)

            def inverse_deviation(before, t):
                v.wait_ge(x_std_ready, before + (t + 1))
                v.reciprocal(x_rs[:, t:t + 1], x_std[:, t:t + 1])
                v.drain()

            def norm_tile(l, which, name, t):
                if t == 0:
                    v.wait_ge(norm_rows, l * 64 + 32 * (which + 1))
                if t >= 2:
                    v.wait_ge(unit_ready, unit_value(l, name, 2 * (t - 2) + 1))
                    if which == 1:
                        v.wait_ge(row_stored[t % 2], l * 160 + 16)
                inverse_deviation(l * 8 + 4 * which, t)
                v.scalar_tensor_tensor(h_nat[:, t % 2], x[:, t], x_rs[:, t:t + 1], scale_row[:], ALU.mult, ALU.mult)
                v.drain()
                v.tensor_tensor(h_nat[:, t % 2], h_nat[:, t % 2], shift_row[:], ALU.add).then_inc(h_ready, 1)

            def norm_lo(l, name, t):
                for j in range(2):
                    unit_lo_half(l, name, 2 * t + j, hT_hi, hT_lo, t, j)

            def unit_lo_half(l, name, n, dst_hi, dst_lo, t, j):
                bank = 4 + (UNIT0[name] + n) % 2
                v.wait_ge(unit_hi, l * NSPLIT + (SPLIT0[name] + n + 1))
                where = (slice(None), slice(4 * j, 4 * j + 4), slice(t * P, (t + 1) * P))
                v.tensor_tensor(dst_lo[where], ps[:, bank].rearrange("p (a b) -> p a b", a=4), dst_hi[where],
                                ALU.subtract).then_inc(unit_free, 1)

            def acc_wait(l, g, t):
                if t < 3:
                    v.wait_ge(acc_ready, l * (3 * NGROUP) + (3 * g + t + 1))
                else:
                    v.wait_ge(w_used, w_done(l, LAST[NAMES[g]]))

            def read_group(l, g):
                name = NAMES[g]
                for t in range(NT):
                    if name in ("q", "k"):
                        dst = (q_rot if name == "q" else k_rot)[:, t]
                        if name == "q" and t == 0:
                            v.wait_ge(rope_landed, l * 16 + 16)
                        acc_wait(l, g, t)
                        a4 = ps[:, t].rearrange("p (h d) -> p h d", h=HEADS)
                        b4 = tmp[:, t % 2].rearrange("p (h d) -> p h d", h=HEADS)
                        cos = rope[:, 0, t].unsqueeze(1)
                        sin = rope[:, 1, t].unsqueeze(1)
                        v.tensor_tensor(dst.rearrange("p (h d) -> p h d", h=HEADS), a4, cos.broadcast_to([P, HEADS, DK]), ALU.mult)
                        v.tensor_tensor(b4[:, :, 0:64], a4[:, :, 64:128], sin[:, :, 0:64].broadcast_to([P, HEADS, 64]), ALU.mult)
                        v.tensor_tensor(b4[:, :, 64:128], a4[:, :, 0:64], sin[:, :, 64:128].broadcast_to([P, HEADS, 64]),
                                        ALU.mult).then_inc(acc_free, 1)
                        v.drain()
                        v.tensor_tensor(dst, dst, tmp[:, t % 2], ALU.add).then_inc(rot_done, 1)
                    elif name in ("g0", "g1"):
                        pair = int(name[1])
                        acc_wait(l, g, t)
                        v.wait_ge(gate_sig, l * 8 + (4 * pair + t + 1))
                        v.tensor_tensor(tmp[:, t % 2], tmp[:, t % 2], ps[:, t], ALU.mult).then_inc(acc_free, 1)
                        v.drain()
                        for j in range(2):
                            h = 2 * pair + j
                            yh = y[:, t, h * DV:(h + 1) * DV]
                            one = v.scalar_tensor_tensor(yh, yh, y_rs[:, 4 * h + t:4 * h + t + 1],
                                                         tmp[:, t % 2, j * DV:(j + 1) * DV], ALU.mult, ALU.mult)
                        one.then_inc(gated, 1)
                    elif name in ("P0", "P1"):
                        acc_wait(l, g, t)
                        v.wait_ge(acc_free, acc_value(l, g - 1, t))
                        m = merged[:, int(name[1]), t]
                        v.tensor_tensor(m, m, ps[:, t], ALU.mult).then_inc(acc_free, 1)
                    elif name in ("R0", "R1"):
                        acc_wait(l, g, t)
                        v.wait_ge(acc_free, acc_value(l, g - 1, t))
                        m = merged[:, int(name[1]), t]
                        v.tensor_tensor(sig_ret[:, t], sig_ret[:, t], ps[:, t], ALU.mult).then_inc(acc_free, 1)
                        v.drain()
                        v.tensor_tensor(m, m, sig_ret[:, t], ALU.add).then_inc(merged_add, 1)

            def read_output(l, half, t):
                if half == 0 and t == 0:
                    v.wait_ge(x_back, l * 16 + 16)
                    v.wait_ge(gate_landed, l * 32 + 16)
                acc_wait(l, NGROUP - 2 + half, t)
                cols = slice(512 * half, 512 * half + 512)
                v.tensor_tensor(tmp[:, t % 2], ps[:, t], gate_row[:, cols], ALU.mult).then_inc(acc_free, 1)
                v.drain()
                v.tensor_tensor(x[:, t, cols], x[:, t, cols], tmp[:, t % 2], ALU.add).then_inc(x_added, 1)

            def retention_pair(l, h0):
                def mask(h):
                    v.wait_ge(score_ready, l * HEADS + (h + 1))
                    v.tensor_tensor(scores[:, h % 2].rearrange("p (n c) -> p n c", n=NT),
                                    ps[:, 4 + h % 2].rearrange("p (n c) -> p n c", n=NT),
                                    k("causal").unsqueeze(1).broadcast_to([P, NT, P]), ALU.mult).then_inc(score_masked, 1)

                def kv(h):
                    for n in range(3):
                        i = 3 * h + n
                        if n != 1:
                            v.wait_ge(kv_ready, l * 8 + (2 * h + n // 2 + 1))
                        v.wait_ge(state_ready, l * 12 + (i + 1))
                        if n == 0:
                            v.tensor_copy(kv_sum[:, 0], ps[:, 6, 0:DV]).then_inc(kv_used, 1)
                        else:
                            src = ps[:, 6, DV:2 * DV] if n == 1 else ps[:, 0, 0:DV]
                            v.scalar_tensor_tensor(kv_sum[:, n], kv_sum[:, n - 1], GAMMA_C[h], src, ALU.mult,
                                                   ALU.add).then_inc(kv_used, 1)
                        v.drain()

                def y_tiles(h, part, bank):
                    v.wait_ge(y_ready, l * 8 + (2 * h + part + 1))
                    for n in (2 * part, 2 * part + 1):
                        v.tensor_scalar(y[:, n, h * DV:(h + 1) * DV], ps[:, bank, DV * (n % 2):DV * (n % 2) + DV],
                                        k("xi")[:, h:h + 1], None, ALU.mult).then_inc(y_read, 1)

                mask(h0)
                kv(h0)
                mask(h0 + 1)
                y_tiles(h0, 0, 1)
                y_tiles(h0, 1, 2)
                kv(h0 + 1)
                y_tiles(h0 + 1, 0, 3)
                y_tiles(h0 + 1, 1, 1)

            def head_scales(l, pair):
                v.wait_ge(y_std_ready, l * 2 + (pair + 1))
                v.reciprocal(y_rs[:, 8 * pair:8 * pair + 8], y_std[:, 8 * pair:8 * pair + 8])
                v.drain()

            def misc(l, name):
                if name == "v0":
                    for which, dst in (("q", qT), ("k", kT)):
                        for t in range(NT):
                            v.wait_ge(unit_ready, unit_value(l, which, t))
                            v.tensor_copy(dst[:, :, t * P:(t + 1) * P],
                                          ps[:, 4 + (UNIT0[which] + t) % 2].rearrange("p (a b) -> p a b", a=HEADS)
                                          ).then_inc(unit_free, 1)
                elif name == "u":
                    retention_pair(l, 0)
                    for g in range(4):
                        v.wait_ge(unit_ready, unit_value(l, "mix", g))
                        v.tensor_copy(mixT[:, g], ps[:, 4 + (UNIT0["mix"] + g) % 2]).then_inc(unit_free, 1)
                    retention_pair(l, 2)
                    head_scales(l, 0)
                    head_scales(l, 1)
                elif name == "ap0":
                    for t in range(NT):
                        for j in range(2):
                            unit_lo_half(l, "y", 2 * t + j, yT_hi, yT_lo, t, j)
                    for g in range(4):
                        v.wait_ge(unit_hi, l * NSPLIT + (SPLIT0["pw"] + g + 1))
                        v.scalar_tensor_tensor(ypT_lo[:, g], ps[:, 4 + (UNIT0["pw"] + g) % 2], pscale[:, g:g + 1],
                                               ypT_hi[:, g], ALU.mult, ALU.subtract).then_inc(unit_free, 1)
                elif name == "ar1":
                    for t in range(NT):
                        unit_lo_half(l, "m0", t, hT_hi, hT_lo, t, 0)
                elif name == "R1":
                    for t in range(NT):
                        unit_lo_half(l, "m1", t, hT_hi, hT_lo, t, 1)

            def ada_step(l, g):
                if 1 <= g <= NADA:
                    a = g - 1
                    v.wait_ge(mod_stored[(a + 1) % 2], l * (8 * NADA) + 16 * ((3 + a) // 2 + 1))
                    ada_finish(l * NADA + (4 + a), a in (4, 5, 10, 11))
                if g < NADA:
                    r0 = RAW_OF_ADA[(g, 0)]
                    ada_products(lambda j: v.wait_ge(landed[(r0 + j) % RAW_SLOTS], land_value(l, r0 + j)), r0, g % 2)

            def route_tokens(l):
                lg3 = lg[:].rearrange("p (t e) -> p t e", e=NE)
                pr3 = probs[:].rearrange("p (t e) -> p t e", e=NE)
                pr4 = probs[:].rearrange("p (s e) -> p s e", e=4)
                rt3 = rt[:].rearrange("p (t e) -> p t e", e=NE)
                rt4 = rt[:].rearrange("p (s e) -> p s e", e=4)
                s43 = s4[:].rearrange("p (t g) -> p t g", g=NG)
                s4b3 = s4b[:].rearrange("p (t g) -> p t g", g=NG)
                pairs3 = pairs[:].rearrange("p (a b) -> p a b", b=6)
                pos3 = pos[:].rearrange("p (t e) -> p t e", e=NE)
                ch3 = chosen[:].rearrange("p (t e) -> p t e", e=NE)
                hots = [hot1[:].rearrange("p (t e) -> p t e", e=NE), hot2[:].rearrange("p (t e) -> p t e", e=NE)]

                def wide(a, n=NE):
                    return a.unsqueeze(2).broadcast_to([P, NT, n])

                def tt(dst, a, b, op):
                    one = v.tensor_tensor(dst, a, b, op)
                    v.drain()
                    return one

                def first_largest(dst3, src3, biggest, n, rev):
                    tt(dst3, src3, wide(biggest, n), ALU.is_equal)
                    tt(dst3, dst3, rev.unsqueeze(1).broadcast_to([P, NT, n]), ALU.mult)
                    v.tensor_reduce(r1[:], dst3, AX, ALU.max)
                    v.drain()
                    tt(dst3, dst3, wide(r1[:], n), ALU.is_equal)

                v.wait_ge(logits_ready, l + 1)
                tt(lg3, ps[:, 7, 0:64].rearrange("p (t e) -> p t e", e=NE),
                   k("br").unsqueeze(1).broadcast_to([P, NT, NE]), ALU.add)
                v.tensor_reduce(r1[:], lg3, AX, ALU.max)
                v.drain()
                v.tensor_tensor(lg3, lg3, wide(r1[:]), ALU.subtract).then_inc(max_off, 1)
                v.wait_ge(exp_done, l + 1)
                v.tensor_reduce(r1[:], pr3, AX, ALU.add)
                v.drain()
                v.reciprocal(top[:, 0:4], r1[:])
                v.drain()
                tt(pr3, pr3, wide(top[:, 0:4]), ALU.mult)
                v.tensor_tensor(pairs3[:, :, 0:3], pr4[:, :, 0:3], pr4[:, :, 1:4], ALU.add)
                v.tensor_tensor(pairs3[:, :, 3:5], pr4[:, :, 0:2], pr4[:, :, 2:4], ALU.add)
                tt(pairs3[:, :, 5:6], pr4[:, :, 0:1], pr4[:, :, 3:4], ALU.add)
                v.tensor_reduce(s4[:], pairs3, AX, ALU.max)
                v.drain()
                v.tensor_reduce(top[:, 0:4], s43, AX, ALU.max)
                v.drain()
                first_largest(s4b3, s43, top[:, 0:4], NG, k("rev4"))
                group = s4b[:].unsqueeze(2).broadcast_to([P, NT * NG, 4])
                tt(rt4, pr4, group, ALU.mult)
                v.tensor_scalar(s4[:], s4b[:], -1.0, None, ALU.add)
                v.drain()
                tt(rt4, rt4, s4[:].unsqueeze(2).broadcast_to([P, NT * NG, 4]), ALU.add)
                v.tensor_reduce(top[:, 0:4], rt3, AX, ALU.max)
                v.drain()
                first_largest(hots[0], rt3, top[:, 0:4], NE, k("rev16"))
                v.scalar_tensor_tensor(rt[:], hot1[:], -4.0, rt[:], ALU.mult, ALU.add)
                v.drain()
                v.tensor_reduce(top[:, 4:8], rt3, AX, ALU.max)
                v.drain()
                first_largest(hots[1], rt3, top[:, 4:8], NE, k("rev16"))
                v.tensor_tensor(chosen[:], hot1[:], hot2[:], ALU.add).then_inc(chosen_ready, 1)
                v.tensor_tensor(r1[:], top[:, 0:4], top[:, 4:8], ALU.add)
                v.drain()
                v.reciprocal(r1[:], r1[:])
                v.drain()
                v.tensor_tensor(wts[:, 0:4], top[:, 0:4], r1[:], ALU.mult)
                v.tensor_tensor(wts[:, 4:8], top[:, 4:8], r1[:], ALU.mult)
                for j in range(2):
                    v.tensor_tensor(hotid[:, 64 * j:64 * j + 64].rearrange("p (t e) -> p t e", e=NE), hots[j],
                                    wide(k("tokid")), ALU.mult)

                for q in range(2):
                    lo(l, MIX + q, RAW_MIX + q)
                v.wait_ge(pos_ready, l + 1)
                v.tensor_copy(pos[:], ps[:, 7, 0:64])
                v.drain()
                for j in range(2):
                    tt(rt3, hots[j], pos3, ALU.mult)
                    v.tensor_reduce(posk[:, 4 * j:4 * j + 4], rt3, AX, ALU.add)
                    v.drain()
                for j in range(2):
                    for t in range(NT):
                        one = v.tensor_scalar(hot[:, j, t], k("iota"), posk[:, 4 * j + t:4 * j + t + 1], None, ALU.is_equal)
                one.then_inc(hot_ready, 1)

                for q in range(2, W_SLOTS):
                    lo(l, MIX + q, RAW_MIX + q)
                v.wait_ge(idx_sum, l + 1)
                v.tensor_copy(idx[:], ps[:, 6, 64:80]).then_inc(idx_ready, 1)
                v.tensor_scalar(ovn[:], ps[:, 7, 64:80], float(CAP), None, ALU.is_gt)
                v.drain()
                for level in range(2, LEVELS):
                    v.scalar_tensor_tensor(ovn[:], ps[:, 7, 64:80], float(level * CAP), ovn[:], ALU.is_gt, ALU.add)
                    v.drain()
                v.memset(ovc[:, 0:16], 0.0)
                v.memset(ovd[:, 0:16], 0.0)
                v.tensor_copy(ovc[:, 16:32], ovn[:])
                v.drain()
                a, b = ovc, ovd
                for s in (1, 2, 4, 8):
                    tt(b[:, 16:32], a[:, 16:32], a[:, 16 - s:32 - s], ALU.add)
                    a, b = b, a
                tt(ov_range_f[:, 0:1], ov_range_f[:, 0:1], ov_range_f[:, 1:2], ALU.add)
                tt(ovd[:, 16:32], ovc[:, 16:32], ovn[:], ALU.subtract)
                v.tensor_copy(ov_range_f[:, 1:2], ovc[:, 31:32])
                v.drain()
                v.tensor_copy(ov_range[:], ov_range_f[:])
                t3 = ovt[:].rearrange("p (b e) -> p b e", e=NE)
                t23 = ovt2[:].rearrange("p (b e) -> p b e", e=NE)
                block_id = k("blockid").unsqueeze(2).broadcast_to([P, NOV, NE])
                v.tensor_tensor(t3, ovd[:, 16:32].unsqueeze(1).broadcast_to([P, NOV, NE]), block_id, ALU.is_le)
                tt(t23, ovc[:, 16:32].unsqueeze(1).broadcast_to([P, NOV, NE]), block_id, ALU.is_gt)
                tt(t3, t3, t23, ALU.mult)
                tt(t3, t3, k("eid").unsqueeze(1).broadcast_to([P, NOV, NE]), ALU.mult)
                v.tensor_reduce(ovt2[:, 0:NOV], t3, AX, ALU.add)
                v.drain()
                v.tensor_copy(ov_expert[:], ovt2[:, 0:NOV])
                v.tensor_scalar(ovd[:, 16:32], ovd[:, 16:32], float(NE - 1), float(CAP), ALU.add, ALU.mult)
                v.drain()
                tt(ovd[:, 16:32], ovd[:, 16:32], k("ecap"), ALU.subtract)
                v.tensor_scalar(rt[:], pos[:], float(CAP), None, ALU.is_ge)
                v.drain()
                tt(rt3, rt3, ovd[:, 16:32].unsqueeze(1).broadcast_to([P, NT, NE]), ALU.mult)
                tt(rt3, rt3, k("ecap").unsqueeze(1).broadcast_to([P, NT, NE]), ALU.add)
                tt(pos3, rt3, pos3, ALU.add)
                for j in range(2):
                    tt(rt3, hots[j], pos3, ALU.mult)
                    v.tensor_reduce(slotf[:, 4 * j:4 * j + 4], rt3, AX, ALU.add)
                    v.drain()
                v.memset(ov_base[:], float(NE * CAP))
                v.tensor_copy(slot_i[:], slotf[:])
                v.drain()
                v.sem_inc(slots_ready, 1)

            def gathered_lo(E, slot):
                for j in range(2):
                    v.wait_ge(xgT_hi_ready, E * 2 + (j + 1))
                    cols = slice(512 * j, 512 * j + 512)
                    v.tensor_tensor(xgT_lo[:, slot, cols], ps[:, 4 + j], xgT_hi[:, slot, cols],
                                    ALU.subtract).then_inc(xgT_lo_ready, 1)

            def expert(l, e, odd, first=False, last=False):
                E = l * NE + e
                q0 = l * PROD + e * EXP

                def lo_e(n):
                    r = 12 * odd + n
                    v.wait_ge(w_hi_ready, q0 + (MIX + n + 1))
                    v.tensor_tensor(w_lo[:, n % W_SLOTS], expert_piece(first, n, r), w_hi[:, n % W_SLOTS],
                                    ALU.subtract).then_inc(raw_used, 1)

                def hidden(half):
                    v.wait_ge(act_sig, E * 2 + (half + 1))
                    s = tmp[:, half, 0:256]
                    v.tensor_tensor(s, s, ps[:, half, 0:256], ALU.mult)
                    v.drain()
                    v.tensor_tensor(hid[:, 256 * half:256 * half + 256], s, ps[:, half, 256:512],
                                    ALU.mult).then_inc(hid_ready, 1)

                def hidT(half):
                    v.wait_ge(hidT_hi_ready, E * 2 + (half + 1))
                    cols = slice(256 * half, 256 * half + 256)
                    v.tensor_tensor(hidT_lo[:, cols], ps[:, 6 + half, 0:256], hidT_hi[:, cols],
                                    ALU.subtract).then_inc(hidT_lo_ready, 1)

                lo_e(4)
                lo_e(5)
                hidden(0)
                lo_e(6)
                lo_e(7)
                hidT(0)
                lo_e(8)
                lo_e(9)
                hidden(1)
                lo_e(10)
                lo_e(11)
                hidT(1)
                if not last:
                    lo_e(12)
                    lo_e(13)
                    gathered_lo(E + 1, 1 - odd)
                    lo_e(14)
                    lo_e(15)
                v.wait_ge(w_used, q0 + (MIX + EXP + W_SLOTS))
                v.wait_ge(row_stored[odd], l * 160 + (e - odd) * 8 + 32)
                for half in range(2):
                    cols = slice(512 * half, 512 * half + 512)
                    one = v.tensor_tensor(y_out[:, odd, cols], ps[:, 2 + half], gate_row[:, cols], ALU.mult)
                one.then_inc(y_copied, 1)

            for q in range(W_SLOTS):
                lo(0, q, RAW_OF_W[q])
            apart(v)
            with v.Fori(0, DEPTH) as l:
                for t in range(NT):
                    norm_tile(l, 0, "h1", t)
                    if t:
                        norm_lo(l, "h1", t - 1)
                norm_lo(l, "h1", NT - 1)
                for q in range(LAST["O0"] + 1):
                    for g in range(NGROUP - 1):
                        if LAST[NAMES[g]] == q:
                            read_group(l, g)
                            if NAMES[g] == "O0":
                                for t in range(NT):
                                    read_output(l, 0, t)
                            misc(l, NAMES[g])
                            ada_step(l, g)
                    lo(l, q + W_SLOTS, RAW_OF_W[q + W_SLOTS])
                read_output(l, 1, 0)
                read_output(l, 1, 1)
                norm_tile(l, 1, "h2", 0)
                read_output(l, 1, 2)
                norm_tile(l, 1, "h2", 1)
                norm_lo(l, "h2", 0)
                read_output(l, 1, 3)
                norm_tile(l, 1, "h2", 2)
                norm_lo(l, "h2", 1)
                norm_tile(l, 1, "h2", 3)
                norm_lo(l, "h2", 2)
                norm_lo(l, "h2", 3)
                route_tokens(l)
                gathered_lo(l * NE, 0)
                v.wait_ge(gate_landed, l * 32 + 32)
                expert(l, 0, 0, first=True)
                expert(l, 1, 1)
                apart(v)
                with v.Fori(1, NE // 2 - 1) as j:
                    expert(l, j * 2, 0)
                    expert(l, j * 2 + 1, 1)
                expert(l, NE - 2, 0)
                expert(l, NE - 1, 1, last=True)

                before, count = overflow_blocks(v, l)
                with v.If(count > 0):
                    v.wait_ge(w_used, l * PROD + (PROD + W_SLOTS))
                    apart(v)
                    with v.Fori(0, count) as slot:
                        b = slot + before
                        for j in range(2):
                            for t in range(NT):
                                one = v.tensor_scalar(o_hot[:, 4 * j + t], k("iota"), ov_base[:, 0:1],
                                                      slotf[:, 4 * j + t:4 * j + t + 1], ALU.add, ALU.is_equal)
                        v.drain()
                        v.tensor_scalar(ov_base[:], ov_base[:], float(CAP), None, ALU.add).then_inc(ov_step, 1)
                        v.wait_ge(ov_step, b * OV_STEPS + 2)
                        v.tensor_copy(o_idx[:], ps[:, 6, 0:1]).then_inc(ov_step, 1)
                        v.wait_ge(ov_step, b * OV_STEPS + 4)
                        v.tensor_copy(o_xT[:, 0:4], ps[:, 4].rearrange("p (a b) -> p a b", a=4))
                        v.tensor_copy(o_xT[:, 4:8], ps[:, 5].rearrange("p (a b) -> p a b", a=4)).then_inc(ov_step, 1)
                        v.wait_ge(ov_step, b * OV_STEPS + 14)
                        for half in range(2):
                            v.tensor_tensor(o_sig[:, half], o_sig[:, half], ps[:, half, 0:256], ALU.mult)
                        v.drain()
                        for half in range(2):
                            one = v.tensor_tensor(o_hid[:, 256 * half:256 * half + 256], o_sig[:, half],
                                                  ps[:, half, 256:512], ALU.mult)
                        one.then_inc(ov_step, 1)
                        v.wait_ge(ov_step, b * OV_STEPS + 16)
                        v.tensor_copy(o_hidT[:], ps[:, 6].rearrange("p (a b) -> p a b", a=4)).then_inc(ov_step, 1)
                        v.wait_ge(ov_step, b * OV_STEPS + 21)
                        v.tensor_tensor(o_y[:, 0:512], ps[:, 2], gate_row[:, 0:512], ALU.mult)
                        v.tensor_tensor(o_y[:, 512:1024], ps[:, 3], gate_row[:, 512:1024], ALU.mult).then_inc(ov_step, 1)
                        v.drain()
                v.nop()

                with v.If(l < DEPTH - 1):
                    for q in range(W_SLOTS):
                        lo(l + 1, q, RAW_OF_W[q])
                v.nop()
                for t in range(NT):
                    v.wait_ge(pair_in[t], l * 32 + 32)
                    v.scalar_tensor_tensor(x[:, t], y_pair[:, t, 0], wts[:, t:t + 1], x[:, t], ALU.mult, ALU.add)
                    v.drain()
                    v.scalar_tensor_tensor(x[:, t], y_pair[:, t, 1], wts[:, 4 + t:5 + t], x[:, t], ALU.mult,
                                           ALU.add).then_inc(x_final, 1)

            v.wait_ge(norm_rows, DEPTH * 64 + 48)
            for t in range(NT):
                inverse_deviation(DEPTH * 8, t)
                v.scalar_tensor_tensor(x[:, t], x[:, t], x_rs[:, t:t + 1], scale_row[:], ALU.mult,
                                       ALU.mult).then_inc(norm_done, 1)

        @block.tensor
        def _(pe):
            pe.sem_inc(w_used, W_SLOTS)
            pe.sem_inc(xgT_ready, 2)
            pe.wait_ge(consts_landed, 16)

            def three_passes(dst, a_hi, a_lo, b_hi, b_lo, start, stop):
                pe.matmul(dst, a_lo, b_hi, start=start, stop=False)
                pe.matmul(dst, a_hi, b_lo, start=False, stop=False)
                return pe.matmul(dst, a_hi, b_hi, start=False, stop=stop)

            def product(l, g, j, t):
                name, n = GROUPS[g]
                left_hi, left_lo = {"P": (ypT_hi, ypT_lo), "R": (yT_hi, yT_lo)}.get(name[0], (hT_hi, hT_lo))
                q = FIRST[name] + j
                s = q % W_SLOTS
                if t == 0:
                    pe.wait_ge(raw_used, raw_value(l, RAW_OF_W[q]))
                if j == 0:
                    pe.wait_ge(acc_free, l * (4 * NGROUP) + (4 * g + t + 1))
                for i in range(2):
                    cols = slice(t * P, (t + 1) * P)
                    w_cols = slice(512 * i, 512 * i + 512)
                    mm = three_passes(ps[:, t], left_hi[:, 2 * j + i, cols], left_lo[:, 2 * j + i, cols],
                                      w_hi[:, s, w_cols], w_lo[:, s, w_cols],
                                      j == 0 and i == 0, j == n - 1 and i == 1)
                if j == n - 1 and t < NT - 1:
                    mm.then_inc(acc_ready, 1)
                if t == NT - 1:
                    mm.then_inc(w_used, 1)

            def group(l, g):
                name, n = GROUPS[g]
                if name == "g0":
                    pe.wait_ge(kv_used, l * 12 + (12 + 2))
                    pe.wait_ge(y_read, l * 16 + (16 + 2))
                for j in range(n):
                    for t in range(NT):
                        if name == "R1" and j == 1 and t % 2 == 0:
                            merged_transposes(l, 0, t)
                        if name == "O0":
                            if (j, t) == (0, 0):
                                units_done(l, "m0")
                            elif j == 1 and t % 2 == 0:
                                merged_transposes(l, 1, t)
                            elif (j, t) == (2, 0):
                                units_done(l, "m1")
                        product(l, g, j, t)

            def merged_transposes(l, half, t0):
                for t in (t0, t0 + 1):
                    pe.wait_ge(merged_add, l * 8 + (4 * half + t + 1))
                    transposes(l, ("m0", "m1")[half], t, merged[:, half, t])

            def group_tile(l, g, t):
                for j in range(GROUPS[g][1]):
                    product(l, g, j, t)

            def unit(l, name, n):
                pe.wait_ge(unit_free, l * NUNIT + (UNIT0[name] + n + 1))
                return ps[:, 4 + (UNIT0[name] + n) % 2]

            def units_done(l, name):
                n = UNITS[name]
                pe.wait_ge(unit_free, l * NUNIT + (UNIT0[name] + n + 2))

            def transposes(l, name, n, src):
                bank = unit(l, name, n)
                for i in range(4):
                    one = pe.transpose(bank[:, i * P:(i + 1) * P], src[:, i * P:(i + 1) * P], ident)
                one.then_inc(unit_ready, 1)

            def norm_transposes(l, which, name, t):
                pe.wait_ge(h_ready, l * 8 + (4 * which + t + 1))
                for j in range(2):
                    transposes(l, name, 2 * t + j, h_nat[:, t % 2, 512 * j:512 * j + 512])

            def retention_pair(l, h0):
                def score(h):
                    for n in range(NT):
                        cols = slice(n * P, (n + 1) * P)
                        one = pe.matmul(ps[:, 4 + h % 2, cols], kT[:, h, cols], qT[:, h, cols], start=True, stop=True)
                    one.then_inc(score_ready, 1)

                def kv(h):
                    pe.wait_ge(kv_used, l * 12 + (3 * h + 2))
                    for n in range(2):
                        one = pe.matmul(ps[:, 6, DV * n:DV * n + DV], k_rot[:, n, h * DK:(h + 1) * DK],
                                        y[:, n, h * DV:(h + 1) * DV], start=True, stop=True)
                    one.then_inc(kv_ready, 1)
                    pe.matmul(ps[:, 0, 0:DV], k_rot[:, 2, h * DK:(h + 1) * DK], y[:, 2, h * DV:(h + 1) * DV],
                              start=True, stop=True).then_inc(kv_ready, 1)

                def y_tiles(h, part, bank):
                    if part == 0:
                        pe.wait_ge(score_masked, l * HEADS + (h + 1))
                    for n in (2 * part, 2 * part + 1):
                        dst = ps[:, bank, DV * (n % 2):DV * (n % 2) + DV]
                        one = pe.matmul(dst, scores[:, h % 2, n * P:(n + 1) * P], y[:, n, h * DV:(h + 1) * DV],
                                        start=True, stop=n == 0)
                        if n:
                            pe.wait_ge(state_ready, l * 12 + (3 * h + n + 3))
                            one = pe.matmul(dst, qT[:, h, n * P:(n + 1) * P], state[:, n - 1], start=False, stop=True)
                    one.then_inc(y_ready, 1)

                score(h0)
                score(h0 + 1)
                pe.wait_ge(acc_free, acc_value(l, NAMES.index("u"), NT - 1))
                if h0:
                    pe.wait_ge(y_read, l * 16 + (8 + 2))
                kv(h0)
                y_tiles(h0, 0, 1)
                y_tiles(h0, 1, 2)
                kv(h0 + 1)
                y_tiles(h0 + 1, 0, 3)
                pe.wait_ge(y_read, l * 16 + (4 * h0 + 2 + 2))
                y_tiles(h0 + 1, 1, 1)

            def ada_reduce(a_all, slot):
                pe.wait_ge(ada_mac, a_all + 1)
                if not isinstance(a_all, int) or a_all:
                    pe.wait_ge(ada_row_ready, a_all)
                pe.matmul(ps[0:1, 7], k("ones")[:, 0:1], ada_acc[:, slot], start=True, stop=True).then_inc(ada_sum, 1)

            def misc(l, name):
                if name == "v0":
                    pe.wait_ge(rot_done, l * 8 + 8)
                    for which, src in (("q", q_rot), ("k", k_rot)):
                        for t in range(NT):
                            transposes(l, which, t, src[:, t])
                    units_done(l, "k")
                elif name == "u":
                    retention_pair(l, 0)
                    pe.wait_ge(score_masked, l * HEADS + 2)
                    for g in range(4):
                        bank = unit(l, "mix", g)
                        for t in range(NT):
                            src = u[:, t, g * P:(g + 1) * P]
                            if t == 0:
                                pe.matmul(bank[:, 0:16], src, k("diag0")[:, 16 * g:16 * g + 16], start=True, stop=True)
                                one = pe.matmul(bank[:, 16:P], src, k("diag")[:, g * P + 16:(g + 1) * P], start=True, stop=True)
                            else:
                                pe.matmul(bank[:, t * P:(t + 1) * P], src, k("diag")[:, g * P:(g + 1) * P],
                                          start=True, stop=False)
                                one = pe.matmul(bank[:, t * P:t * P + 16], u[:, t - 1, g * P:(g + 1) * P],
                                                k("off")[:, 16 * g:16 * g + 16], start=False, stop=True)
                        one.then_inc(unit_ready, 1)
                    units_done(l, "mix")
                    retention_pair(l, 2)
                elif name == "ap0":
                    pe.wait_ge(gated, l * 8 + (8 + 2))
                    for t in range(NT):
                        for j in range(2):
                            transposes(l, "y", 2 * t + j, y[:, t, 512 * j:512 * j + 512])
                    pe.wait_ge(pw_landed, l * 32 + 32)
                    for g in range(4):
                        bank = unit(l, "pw", g)
                        pe.matmul(bank, pw[:, g], mixT[:, g], start=True, stop=True).then_inc(unit_ready, 1)
                    units_done(l, "pw")

            def gathered_transposes(E, slot):
                pe.wait_ge(gathered[slot], (E - slot) * 8 + 16)
                for j in range(2):
                    for i in range(4):
                        c = (4 * j + i) * P
                        one = pe.transpose(ps[:, 4 + j, i * P:(i + 1) * P], xg[:, slot, c:c + P], ident)
                    one.then_inc(xgT_ready, 1)

            def expert(l, e, odd, first=False, last=False):
                E = l * NE + e
                q0 = l * PROD + e * EXP
                r0 = l * RAW + e * EXP

                def halves_ready(n):
                    pe.wait_ge(raw_used, r0 + (PRE + RAW_MIX + n + 1 + RAW_SLOTS))

                def gate_up(n):
                    half, j = n // 4, n % 4
                    halves_ready(n)
                    if j % 2 == 0:
                        pe.wait_ge(xgT_lo_ready, E * 2 + (j // 2 + 1))
                    for i in range(2):
                        a = slice((2 * j + i) * P, (2 * j + i + 1) * P)
                        b = slice(512 * i, 512 * i + 512)
                        mm = three_passes(ps[:, half], xgT_hi[:, odd, a], xgT_lo[:, odd, a], w_hi[:, n % W_SLOTS, b],
                                          w_lo[:, n % W_SLOTS, b], j == 0 and i == 0, j == 3 and i == 1)
                    mm.then_inc(w_used, 1)

                def down(n):
                    j = n - 8
                    halves_ready(n)
                    if j == 0:
                        pe.wait_ge(y_copied, E + 1)
                    if j % 2 == 0:
                        pe.wait_ge(hidT_lo_ready, E * 2 + (j // 2 + 1))
                    for i in range(2):
                        a = slice(j * P, (j + 1) * P)
                        b = slice(512 * i, 512 * i + 512)
                        mm = three_passes(ps[:, 2 + i], hidT_hi[:, a], hidT_lo[:, a], w_hi[:, n % W_SLOTS, b],
                                          w_lo[:, n % W_SLOTS, b], j == 0, j == 3)
                    mm.then_inc(w_used, 1)

                def hidden_transposes(half):
                    pe.wait_ge(hid_ready, E * 2 + (half + 1))
                    for i in range(2):
                        c = 256 * half + i * P
                        one = pe.transpose(ps[:, 6 + half, i * P:(i + 1) * P], hid[:, c:c + P], ident)
                    one.then_inc(hidT_ready, 1)

                for n in range(6):
                    gate_up(n)
                hidden_transposes(0)
                gate_up(6)
                gate_up(7)
                down(8)
                down(9)
                hidden_transposes(1)
                if not last:
                    gathered_transposes(E + 1, 1 - odd)
                down(10)
                down(11)

            for a in range(4):
                ada_reduce(a, a % 2)

            apart(pe)
            with pe.Fori(0, DEPTH) as l:
                pe.wait_ge(y_copied, l * NE + 1)
                norm_transposes(l, 0, "h1", 0)
                for t in range(NT):
                    if t + 1 < NT:
                        norm_transposes(l, 0, "h1", t + 1)
                    pe.wait_ge(unit_free, unit_value(l, "h1", 2 * t + 1) + 2)
                    group_tile(l, 0, t)
                for g in range(1, NGROUP - 1):
                    group(l, g)
                    misc(l, NAMES[g])
                    if 1 <= g <= NADA:
                        ada_reduce(l * NADA + (4 + g - 1), (g - 1) % 2)
                for t in range(NT):
                    if t == 3:
                        norm_transposes(l, 1, "h2", 0)
                    group_tile(l, NGROUP - 1, t)
                for half in range(2):
                    for t in ((1, 2), (3,))[half]:
                        norm_transposes(l, 1, "h2", t)
                    pe.wait_ge(unit_free, unit_value(l, "h2", 4 * half + 3) + 2)
                    cols = slice(256 * half, 256 * half + 256)
                    for i in range(8):
                        e = slice(NE * i, NE * i + NE)
                        mm = three_passes(ps[0:NE, 6, cols], wr_hi[:, e], wr_lo[:, e], hT_hi[:, i, cols], hT_lo[:, i, cols],
                                          i == 0, i == 7)
                mm.then_inc(logitsT_ready, 1)
                pe.wait_ge(logitsT_copied, l + 1)
                pe.wait_ge(ada_row_ready, l * NADA + (4 + NADA))
                for t in range(NT):
                    one = pe.matmul(ps[:, 7, NE * t:NE * t + NE], lgT[0:NE, t * P:(t + 1) * P], ident[0:NE, 0:NE],
                                    start=True, stop=True)
                one.then_inc(logits_ready, 1)
                pe.wait_ge(chosen_ready, l + 1)
                pe.matmul(ps[:, 7, 0:NE * NT], before_r[:], chosen[:], start=True, stop=False)
                for s in range(1, NT):
                    pe.matmul(ps[:, 7, NE * s:NE * NT], ones_r[:], chosen[:, 0:NE * (NT - s)], start=False, stop=s == NT - 1)
                for s in range(NT):
                    one = pe.matmul(ps[:, 7, 64:80], ones_r[:], chosen[:, NE * s:NE * s + NE], start=s == 0, stop=s == NT - 1)
                one.then_inc(pos_ready, 1)
                pe.wait_ge(hot_ready, l + 1)
                for j in range(2):
                    for t in range(NT):
                        one = pe.matmul(ps[:, 6, 64:80], hot[:, j, t], hotid[:, 64 * j + NE * t:64 * j + NE * t + NE],
                                        start=j == 0 and t == 0, stop=j == 1 and t == NT - 1)
                one.then_inc(idx_sum, 1)

                pe.wait_ge(acc_free, acc_value(l, NGROUP - 1, NT - 1))
                gathered_transposes(l * NE, 0)
                expert(l, 0, 0, first=True)
                expert(l, 1, 1)
                apart(pe)
                with pe.Fori(1, NE // 2 - 1) as j:
                    expert(l, j * 2, 0)
                    expert(l, j * 2 + 1, 1)
                expert(l, NE - 2, 0)
                expert(l, NE - 1, 1, last=True)

                pe.wait_ge(slots_ready, l + 1)
                before, count = overflow_blocks(pe, l)
                with pe.If(count > 0):
                    pe.wait_ge(y_copied, l * NE + (NE + 1))
                    apart(pe)
                    with pe.Fori(0, count) as slot:
                        b = slot + before
                        pe.wait_ge(ov_step, b * OV_STEPS + 1)
                        for n in range(8):
                            one = pe.matmul(ps[:, 6, 0:1], o_hot[:, n], k("tokid")[:, n % NT:n % NT + 1], start=n == 0, stop=n == 7)
                        one.then_inc(ov_step, 1)
                        pe.wait_ge(ov_x, b * 16 + 16)
                        pe.wait_ge(ov_step, b * OV_STEPS + 3)
                        for i in range(8):
                            one = pe.transpose(ps[:, 4 + i // 4, (i % 4) * P:(i % 4 + 1) * P], o_x[:, i * P:(i + 1) * P], ident)
                        one.then_inc(ov_step, 1)
                        pe.wait_ge(ov_step, b * OV_STEPS + 5)
                        for n in range(EXP):
                            if n == 8:
                                pe.wait_ge(ov_step, b * OV_STEPS + 15)
                                for i in range(4):
                                    one = pe.transpose(ps[:, 6, i * P:(i + 1) * P], o_hid[:, i * P:(i + 1) * P], ident)
                                one.then_inc(ov_step, 1)
                                pe.wait_ge(ov_step, b * OV_STEPS + 17)
                            pe.wait_ge(ov_w, b * (16 * EXP) + (16 * n + 16))
                            for i in range(2):
                                piece = o_w[:, 512 * i:512 * i + 512]
                                if n < 8:
                                    mm = pe.matmul(ps[:, n // 4], o_xT[:, 2 * (n % 4) + i], piece,
                                                   start=n % 4 == 0 and i == 0, stop=n % 4 == 3 and i == 1)
                                else:
                                    mm = pe.matmul(ps[:, 2 + i], o_hidT[:, n - 8], piece, start=n == 8, stop=n == 11)
                            mm.then_inc(ov_step, 1)
                pe.nop()

        @block.gpsimd
        def _(pool):
            pool.dma_start(const[:], consts).then_inc(consts_landed, 16)
            pool.dma_start(cond_raw[:], c_in).then_inc(c_landed, 16)

            def add_load(a_all):
                pool.dma_start(ada_add[:].rearrange("p a n -> p (a n)"), ada_rows[bass.ds(a_all, 1)]).then_inc(ada_add_landed, 16)

            def mod_store(a_all, parity):
                pool.wait_ge(ada_row_ready, a_all + 1)
                apart(pool)
                pool.dma_start(mod[bass.ds(a_all, 1)], ada_row[:]).then_inc(mod_stored[parity], 16)

            for a in range(4):
                if a:
                    pool.wait_ge(ada_row_ready, a)
                apart(pool)
                add_load(a)
                mod_store(a, a % 2)
                if a == 1:
                    pool.dma_start(x[:].rearrange("p t d -> p (t d)"), x_in).then_inc(x_landed, 16)

            def broadcast_rows(dst, first, semaphore):
                src = mod[bass.ds(first, 2)].rearrange("a n -> (a n)").unsqueeze(0).broadcast_to([P, D])
                pool.dma_start(dst[:], src).then_inc(semaphore, 16)

            def expert(l, e, odd, first=False, last=False):
                E = l * NE + e
                if not last:
                    pool.wait_ge(xgT_ready, E * 2 + 2)
                    apart(pool)
                    pool.tensor_copy(idx_next[:, 1 - odd:2 - odd], idx[:, bass.ds(e + 1, 1)])
                    pool.drain()
                    pool.indirect_dma_start(xg[:, 1 - odd], None, h_rows,
                                            bass.IndirectOffsetOnAxis(ap=idx_next[:, 1 - odd:2 - odd], axis=0)
                                            ).then_inc(gathered[1 - odd], 16)
                pool.wait_ge(y_copied, E + 2)
                apart(pool)
                pool.dma_start(y_rows[bass.ds(e * CAP, CAP)], y_out[0:CAP, odd]).then_inc(row_stored[odd], 16)

            apart(pool)
            for p in range(2):
                pool.wait_ge(mod_stored[p], 32)
            broadcast_rows(shift_row, 0, norm_rows)
            broadcast_rows(scale_row, 2, norm_rows)
            with pool.Fori(0, DEPTH) as l:
                pool.wait_ge(x_final, l * NT + NT)
                apart(pool)
                pool.dma_start(x_state, x[:].rearrange("p t d -> p (t d)")).then_inc(x_saved, 16)
                pool.dma_start(pw[:].rearrange("p g d -> p (g d)"), pool_w[bass.ds(l, 1)].rearrange("o p n -> (o p) n")).then_inc(pw_landed, 16)
                pool.dma_start(pscale[:], pool_scale[bass.ds(l, 1)].rearrange("o p n -> (o p) n")).then_inc(pw_landed, 16)
                pool.wait_ge(h_ready, l * 8 + 4)
                pool.wait_ge(x_saved, l * 16 + 16)
                apart(pool)
                pool.dma_start(rope[:].rearrange("p a t d -> p (a t d)"), rotary).then_inc(rope_landed, 16)
                for n in range(0, NOV * CAP, T):
                    rows = min(T, NOV * CAP - n)
                    first = NE * CAP + n
                    pool.dma_start(y_rows[first:first + rows], x_state.rearrange("p (t d) -> (p t) d", d=D)[0:rows]
                                   ).then_inc(y_filled, 16)
                for a in range(NADA):
                    a_all = l * NADA + (4 + a)
                    pool.wait_ge(ada_row_ready, a_all)
                    apart(pool)
                    add_load(a_all)
                    mod_store(a_all, a % 2)
                    if a == 1:
                        for p in range(2):
                            pool.wait_ge(mod_stored[p], l * 96 + 48)
                        apart(pool)
                        broadcast_rows(gate_row, l * NADA + 4, gate_landed)
                    if a == 5:
                        for p in range(2):
                            pool.wait_ge(mod_stored[p], l * 96 + 80)
                        apart(pool)
                        broadcast_rows(shift_row, l * NADA + 6, norm_rows)
                        broadcast_rows(scale_row, l * NADA + 8, norm_rows)
                pool.wait_ge(unit_ready, l * NUNIT + (UNIT0["m1"] + 4))
                apart(pool)
                pool.dma_start(x[:].rearrange("p t d -> p (t d)"), x_state).then_inc(x_back, 16)
                for t in range(NT):
                    pool.wait_ge(h_ready, l * 8 + (4 + t + 1))
                    apart(pool)
                    pool.dma_start(h_rows[t * P:(t + 1) * P], h_nat[:, t % 2]).then_inc(row_stored[t % 2], 16)
                pool.wait_ge(x_added, l * 8 + 8)
                for p in range(2):
                    pool.wait_ge(mod_stored[p], l * 96 + 96)
                apart(pool)
                broadcast_rows(gate_row, l * NADA + 10, gate_landed)
                broadcast_rows(shift_row, l * NADA + NADA, norm_rows)
                broadcast_rows(scale_row, l * NADA + (NADA + 2), norm_rows)
                for p in range(2):
                    pool.wait_ge(row_stored[p], l * 160 + 32)
                pool.wait_ge(idx_ready, l + 1)
                apart(pool)
                pool.indirect_dma_start(xg[:, 0], None, h_rows, bass.IndirectOffsetOnAxis(ap=idx[:, 0:1], axis=0)
                                        ).then_inc(gathered[0], 16)
                expert(l, 0, 0, first=True)
                expert(l, 1, 1)
                apart(pool)
                with pool.Fori(1, NE // 2 - 1) as j:
                    expert(l, j * 2, 0)
                    expert(l, j * 2 + 1, 1)
                expert(l, NE - 2, 0)
                expert(l, NE - 1, 1, last=True)
                for p in range(2):
                    pool.wait_ge(row_stored[p], l * 160 + 160)
                pool.wait_ge(y_filled, l * FILLS + FILLS)
                apart(pool)

                pool.wait_ge(slots_ready, l + 1)
                before, count = overflow_blocks(pool, l)
                with pool.If(count > 0):
                    apart(pool)
                    with pool.Fori(0, count) as slot:
                        b = slot + before
                        e = pool.value_load(ov_expert[0:1, bass.ds(slot, 1)], min_val=0, max_val=NE - 1)
                        pool.wait_ge(ov_step, b * OV_STEPS + 3)
                        apart(pool)
                        pool.indirect_dma_start(o_x[:], None, h_rows, bass.IndirectOffsetOnAxis(ap=o_idx[:, 0:1], axis=0)
                                                ).then_inc(ov_x, 16)
                        for n in range(EXP):
                            pool.wait_ge(ov_step, b * OV_STEPS + (5 + n if n < 8 else 17 + n - 8))
                            apart(pool)
                            pool.dma_start(o_w[:], w[bass.ds(l * RAW + e * EXP + (PRE + RAW_MIX + n), 1)].rearrange("o p n -> (o p) n")
                                           ).then_inc(ov_w, 16)
                        pool.wait_ge(ov_step, b * OV_STEPS + OV_STEPS)
                        apart(pool)
                        pool.dma_start(y_rows[bass.ds(slot * CAP + NE * CAP, CAP)], o_y[0:CAP]).then_inc(ov_y, 16)
                        pool.wait_ge(ov_y, b * 16 + 16)
                apart(pool)
                pool.nop()

                for t in range(NT):
                    for j in range(2):
                        pool.indirect_dma_start(y_pair[:, t, j], None, y_rows,
                                                bass.IndirectOffsetOnAxis(ap=slot_i[:, 4 * j + t:4 * j + t + 1], axis=0)
                                                ).then_inc(pair_in[t], 16)

            pool.wait_ge(norm_rows, DEPTH * 64 + 32)
            pool.dma_start(scale_row[:], final_g.broadcast_to([P, D])).then_inc(norm_rows, 16)
            for t in range(NT):
                pool.wait_ge(norm_done, t + 1)
                apart(pool)
                pool.dma_start(out[t * P:(t + 1) * P], x[:, t]).then_inc(out_stored, 16)
            pool.wait_ge(out_stored, 16 * NT)
            for p in range(2):
                pool.wait_ge(mod_stored[p], 8 * (4 + DEPTH * NADA))


def weight_stream(w_ada, w_in, w_ret_o, w_pool_o, w_out, w_gate, w_up, w_down):
    out = np.empty((PIECES, P, 1024), np.float32)

    def rows(m, j, c):
        return m[256 * j:256 * j + 256, 512 * c:512 * c + 512].reshape(2, P, 512).transpose(1, 0, 2).reshape(P, 1024)

    n = 0
    for c in range(4):
        for j in range(ADA_PIECES):
            out[n] = rows(w_ada[0], j, c)
            n += 1
    group_of = [g for g, m in GROUPS for _ in range(m)]
    for l in range(DEPTH):
        for s in STREAM:
            if s[0] == "ada":
                a, j = s[1:]
                layer, c = (l, 4 + a) if a < 8 else (min(l + 1, DEPTH - 1), a - 8)
                out[n] = rows(w_ada[layer], j, c)
            else:
                g = group_of[s[1]]
                j = s[1] - FIRST[g]
                m, c = {"P": (w_pool_o, int(g[-1] == "1")), "R": (w_ret_o, int(g[-1] == "1")),
                        "O": (w_out, int(g[-1] == "1"))}.get(g[0], (w_in, W_IN_COLUMN.get(g)))
                out[n] = rows(m[l], j, c)
            n += 1
        for e in range(NE):
            for half in range(2):
                cols = slice(256 * half, 256 * half + 256)
                for j in range(4):
                    r = slice(256 * j, 256 * j + 256)
                    both = np.stack([w_gate[l, e, r, cols], w_up[l, e, r, cols]], 1)
                    out[n] = both.reshape(2, P, 512).transpose(1, 0, 2).reshape(P, 1024)
                    n += 1
            out[n:n + 4] = w_down[l, e].reshape(4, P, 1024)
            n += 4
    assert n == PIECES
    return out


def kernel(x, c, w_ada, b_ada, norm1_g, norm2_g, w_in, w_ret_o, pool_w, pool_scale, w_pool_o, w_out,
           w_router, b_router, w_e_gate, w_e_up, w_e_down, final_g):
    import concourse.bacc as bacc
    from concourse.bass_utils import run_bass_kernel_spmd

    f = [np.asarray(a) for a in (x, c, w_ada, b_ada, norm1_g, norm2_g, w_in, w_ret_o, pool_w, pool_scale, w_pool_o,
                                 w_out, w_router, b_router, w_e_gate, w_e_up, w_e_down, final_g)]
    (x, c, w_ada, b_ada, norm1_g, norm2_g, w_in, w_ret_o, pool_w, pool_scale, w_pool_o, w_out, w_router, b_router,
     w_e_gate, w_e_up, w_e_down, final_g) = f

    consts = constants()
    o, n = CONST_AT["wr"]
    consts[:, o:o + n] = w_router.reshape(8, P, NE).transpose(1, 0, 2).reshape(P, n)
    o, n = CONST_AT["br"]
    consts[:, o:o + n] = b_router[None, :]
    ada_rows = np.zeros((4 + DEPTH * NADA, 2, 512), np.float32)
    for a in range(4 + DEPTH * NADA):
        l, col = divmod(a, NADA)
        if l == DEPTH:
            l = DEPTH - 1
        ada_rows[a, 0] = b_ada[l, 512 * col:512 * col + 512]
        if col in (2, 3):
            ada_rows[a, 1] = norm1_g[l, 512 * (col - 2):512 * (col - 1)]
        if col in (8, 9):
            ada_rows[a, 1] = norm2_g[l, 512 * (col - 8):512 * (col - 7)]
    arrays = {
        "w": weight_stream(w_ada, w_in, w_ret_o, w_pool_o, w_out, w_e_gate, w_e_up, w_e_down),
        "x_in": np.ascontiguousarray(x.reshape(NT, P, D).transpose(1, 0, 2).reshape(P, NT * D)),
        "c_in": np.ascontiguousarray(c.reshape(8, P).T),
        "consts": consts,
        "rotary": rotary_tables().reshape(P, 2 * NT * DK),
        "ada_rows": ada_rows.reshape(-1, 1024),
        "pool_w": np.ascontiguousarray(pool_w.transpose(0, 2, 1, 3).reshape(DEPTH, P, 512)),
        "pool_scale": np.ascontiguousarray(pool_scale.reshape(DEPTH, 4, P).transpose(0, 2, 1)),
        "final_g": np.ascontiguousarray(final_g.reshape(1, D)),
    }
    nc = bacc.Bacc("TRN2", target_bir_lowering=False, num_devices=1)
    args = [nc.dram_tensor(name, a.shape, mybir.dt.from_np(a.dtype), kind="ExternalInput").ap()
            for name, a in arrays.items()]
    out = nc.dram_tensor("out", (T, D), F32, kind="ExternalOutput").ap()
    build(nc, *args, out)
    r = run_bass_kernel_spmd(nc, [arrays], core_ids=[0])
    return r.results[0]["out"].reshape(1, T, D)
```
